# Optimizing a Trainium2 kernel written in Bass

```python
import jax, jax.numpy as jnp
from jax import lax
import numpy as np

D_MODEL = 1024
BATCH = 1
SEQ = 4096
DEPTH = 1
DEC_BATCH = 1
DEC_SEQ = 64
PAST_LEN = 1024

CHUNK = 64
EPS = 1e-6
GLA_HEADS = 4
GLA_DK = 64
GLA_DV = 128
GLA_WIDTH = GLA_HEADS * GLA_DV
GLA_LOWRANK = 16
GLA_TAU = 16.0
GLA_BLOCK = 16
SWA_HEADS = 8
SWA_KV_HEADS = 2
SWA_GROUP = SWA_HEADS // SWA_KV_HEADS
SWA_HD = 64
SWA_WIDTH = SWA_HEADS * SWA_HD
SWA_WINDOW = 128
WIN_CHUNKS = SWA_WINDOW // CHUNK
ROPE_DIM = SWA_HD // 4
ROPE_THETA = 500000.0
MIX_WIDTH = GLA_WIDTH + SWA_WIDTH
SPLITS = [GLA_HEADS * GLA_DK, GLA_HEADS * GLA_DK, GLA_WIDTH, GLA_WIDTH, GLA_LOWRANK,
          SWA_HEADS * SWA_HD, SWA_KV_HEADS * SWA_HD, SWA_KV_HEADS * SWA_HD, SWA_WIDTH]
SPLIT_IDX = [int(i) for i in np.cumsum(SPLITS)[:-1]]
IN_WIDTH = int(sum(SPLITS))

kernel_name = "hymba_gla_swa_sink_stream_step"

def rmsnorm(x, g):
    x32 = x.astype(jnp.float32)
    y = x32 * lax.rsqrt(jnp.mean(x32 * x32, axis=-1, keepdims=True) + EPS)
    return (y * g.astype(jnp.float32)).astype(x.dtype)

def rope_partial(x, pos):
    half = ROPE_DIM // 2
    inv = ROPE_THETA ** (-jnp.arange(half, dtype=jnp.float32) * 2.0 / ROPE_DIM)
    ang = pos.astype(jnp.float32)[:, None] * inv[None, :]
    cos = jnp.cos(ang)[None, :, None, :]
    sin = jnp.sin(ang)[None, :, None, :]
    x1 = x[..., :half].astype(jnp.float32)
    x2 = x[..., half:ROPE_DIM].astype(jnp.float32)
    rot = jnp.concatenate([x1 * cos - x2 * sin, x2 * cos + x1 * sin], axis=-1).astype(x.dtype)
    return jnp.concatenate([rot, x[..., ROPE_DIM:]], axis=-1)

def gla_recurrence(q, k, v, log_a, S0):
    B, T, H, DK = q.shape
    L = GLA_BLOCK
    n = -(-T // L)
    pad = n * L - T
    def blocks(a):
        a = jnp.pad(a.astype(jnp.float32), ((0, 0), (0, pad), (0, 0), (0, 0)))
        return a.reshape(B, n, L, H, a.shape[-1]).transpose(1, 0, 3, 2, 4)
    qb, kb, vb, ab = blocks(q), blocks(k), blocks(v), blocks(log_a)
    b = jnp.cumsum(ab, axis=-2)
    b_end = b[..., -1, :]
    q_in = qb * jnp.exp(b)
    k_in = kb * jnp.exp(-b)
    k_out = kb * jnp.exp(b_end[..., None, :] - b)
    causal = jnp.tril(jnp.ones((L, L), jnp.float32))

    def step(S, inp):
        qi, ki, ko, vi, be = inp
        inter = jnp.einsum('bhld,bhde->bhle', qi, S)
        A = jnp.einsum('bhld,bhmd->bhlm', qi, ki) * causal
        intra = jnp.einsum('bhlm,bhme->bhle', A, vi)
        S_new = jnp.exp(be)[..., None] * S + jnp.einsum('bhld,bhle->bhde', ko, vi)
        return S_new, inter + intra

    S, o = lax.scan(step, S0.astype(jnp.float32), (q_in, k_in, k_out, vb, b_end))
    o = o.transpose(1, 0, 3, 2, 4).reshape(B, n * L, H, v.shape[-1])[:, :T]
    return o.astype(v.dtype), S.astype(S0.dtype)

def chunk_window_mask(qpos, kpos):
    qc = qpos // CHUNK
    kc = kpos // CHUNK
    return (kpos >= 0) & (kc <= qc) & (kc > qc - WIN_CHUNKS)

def sink_attention(q, k, v, mask, sinks):
    s = jnp.einsum('bnqhgd,bnkhd->bnhgqk', q, k).astype(jnp.float32) * (SWA_HD ** -0.5)
    s = jnp.where(mask[None, :, None, None], s, jnp.float32(-1e30))
    sink = jnp.broadcast_to(sinks.astype(jnp.float32).reshape(SWA_KV_HEADS, SWA_GROUP)[:, :, None, None],
                            s.shape[:-1] + (1,))
    p = jax.nn.softmax(jnp.concatenate([s, sink], axis=-1), axis=-1)[..., :-1]
    return jnp.einsum('bnhgqk,bnkhd->bnqhgd', p.astype(v.dtype), v)

def layer(x, c, pos0, S0, k_cache, v_cache, w_ada, b_ada, g_pre, g_post, w_in,
          w_alpha, b_alpha, gla_norm_g, swa_sinks, w_out):
    B, T, _ = x.shape
    shift, scale, gate = jnp.split(jax.nn.silu(c) @ w_ada + b_ada, 3, axis=-1)
    h = rmsnorm(x, g_pre) * (1.0 + scale[:, None, :]) + shift[:, None, :]
    proj = h @ w_in
    gq, gk, gv, gg, ga, sq, sk, sv, sg = jnp.split(proj, SPLIT_IDX, axis=-1)

    q = gq.reshape(B, T, GLA_HEADS, GLA_DK) * (GLA_DK ** -0.5)
    k = gk.reshape(B, T, GLA_HEADS, GLA_DK)
    v = gv.reshape(B, T, GLA_HEADS, GLA_DV)
    log_a = jax.nn.log_sigmoid((ga @ w_alpha + b_alpha).astype(jnp.float32)) / GLA_TAU
    log_a = log_a.reshape(B, T, GLA_HEADS, GLA_DK)
    o_gla, S_new = gla_recurrence(q, k, v, log_a, S0)
    o_gla = rmsnorm(o_gla, gla_norm_g).reshape(B, T, GLA_WIDTH) * jax.nn.silu(gg)

    pos = pos0 + jnp.arange(T, dtype=jnp.int32)
    q = rope_partial(sq.reshape(B, T, SWA_HEADS, SWA_HD), pos)
    k = rope_partial(sk.reshape(B, T, SWA_KV_HEADS, SWA_HD), pos)
    v = sv.reshape(B, T, SWA_KV_HEADS, SWA_HD)
    if k_cache is None:
        nC = T // CHUNK
        qb = q.reshape(B, nC, CHUNK, SWA_KV_HEADS, SWA_GROUP, SWA_HD)
        def band(a):
            ac = a.reshape(B, nC, CHUNK, SWA_KV_HEADS, SWA_HD)
            parts = []
            for s in range(WIN_CHUNKS - 1, -1, -1):
                parts.append(ac if s == 0 else
                             jnp.pad(ac, ((0, 0), (s, 0), (0, 0), (0, 0), (0, 0)))[:, :nC])
            return jnp.concatenate(parts, axis=2)
        qpos = jnp.arange(T, dtype=jnp.int32).reshape(nC, CHUNK)
        kpos = ((jnp.arange(nC, dtype=jnp.int32)[:, None] - (WIN_CHUNKS - 1)) * CHUNK
                + jnp.arange(WIN_CHUNKS * CHUNK, dtype=jnp.int32)[None, :])
        mask = chunk_window_mask(qpos[:, :, None], kpos[:, None, :])
        o_swa = sink_attention(qb, band(k), band(v), mask, swa_sinks)
        W = min(SWA_WINDOW, T)
        new_k, new_v = k[:, T - W:], v[:, T - W:]
    else:
        W = k_cache.shape[1]
        k_all = jnp.concatenate([k_cache.astype(k.dtype), k], axis=1)
        v_all = jnp.concatenate([v_cache.astype(v.dtype), v], axis=1)
        qpos = pos
        kpos = pos0 - W + jnp.arange(W + T, dtype=jnp.int32)
        mask = chunk_window_mask(qpos[:, None], kpos[None, :])[None]
        qb = q.reshape(B, 1, T, SWA_KV_HEADS, SWA_GROUP, SWA_HD)
        o_swa = sink_attention(qb, k_all[:, None], v_all[:, None], mask, swa_sinks)
        new_k, new_v = k_all[:, T:], v_all[:, T:]
    o_swa = o_swa.reshape(B, T, SWA_WIDTH) * jax.nn.silu(sg)

    o = jnp.concatenate([o_gla, o_swa], axis=-1) @ w_out
    y = x + gate[:, None, :] * rmsnorm(o, g_post)
    return y, S_new, new_k, new_v

def setup_inputs(seed: int = 0) -> dict:
    key = jax.random.key(seed)
    ks = jax.random.split(key, 20)
    def nrm(k, shape, s):
        return jax.random.normal(k, shape, jnp.float32) * s
    swa_cache = min(SWA_WINDOW, PAST_LEN)
    return {
        "x_prompt": nrm(ks[0], (BATCH, SEQ, D_MODEL), 1.0),
        "x_sample": nrm(ks[1], (DEC_BATCH, DEC_SEQ, D_MODEL), 1.0),
        "c_prompt": nrm(ks[2], (BATCH, D_MODEL), 1.0),
        "c_sample": nrm(ks[3], (DEC_BATCH, D_MODEL), 1.0),
        "state_gla": nrm(ks[4], (DEPTH, DEC_BATCH, GLA_HEADS, GLA_DK, GLA_DV), 0.5),
        "cache_swa_k": nrm(ks[5], (DEPTH, DEC_BATCH, swa_cache, SWA_KV_HEADS, SWA_HD), 1.0),
        "cache_swa_v": nrm(ks[6], (DEPTH, DEC_BATCH, swa_cache, SWA_KV_HEADS, SWA_HD), 1.0),
        "w_ada": nrm(ks[7], (DEPTH, D_MODEL, 3 * D_MODEL), D_MODEL ** -0.5),
        "b_ada": nrm(ks[8], (DEPTH, 3 * D_MODEL), 0.02),
        "g_pre": 1.0 + nrm(ks[9], (DEPTH, D_MODEL), 0.05),
        "g_post": 1.0 + nrm(ks[10], (DEPTH, D_MODEL), 0.05),
        "w_in": nrm(ks[11], (DEPTH, D_MODEL, IN_WIDTH), D_MODEL ** -0.5),
        "w_alpha": nrm(ks[12], (DEPTH, GLA_LOWRANK, GLA_HEADS * GLA_DK), GLA_LOWRANK ** -0.5),
        "b_alpha": nrm(ks[13], (DEPTH, GLA_HEADS * GLA_DK), 0.5),
        "gla_norm_g": 1.0 + nrm(ks[14], (DEPTH, GLA_DV), 0.05),
        "swa_sinks": nrm(ks[15], (DEPTH, SWA_HEADS), 1.0),
        "w_out": nrm(ks[16], (DEPTH, MIX_WIDTH, D_MODEL), MIX_WIDTH ** -0.5),
    }

def reference(x_prompt, x_sample, c_prompt, c_sample, state_gla, cache_swa_k, cache_swa_v,
              w_ada, b_ada, g_pre, g_post, w_in, w_alpha, b_alpha, gla_norm_g, swa_sinks, w_out):
    Bp = x_prompt.shape[0]
    yp, ys = x_prompt, x_sample
    sp_list, kp_list, vp_list, ss_list, ks_list, vs_list = [], [], [], [], [], []
    for l in range(DEPTH):
        params = (w_ada[l], b_ada[l], g_pre[l], g_post[l], w_in[l], w_alpha[l], b_alpha[l],
                  gla_norm_g[l], swa_sinks[l], w_out[l])
        S0p = jnp.zeros((Bp, GLA_HEADS, GLA_DK, GLA_DV), x_prompt.dtype)
        yp, sp, kp, vp = layer(yp, c_prompt, 0, S0p, None, None, *params)
        ys, ss, kss, vss = layer(ys, c_sample, PAST_LEN, state_gla[l], cache_swa_k[l], cache_swa_v[l], *params)
        sp_list.append(sp); kp_list.append(kp); vp_list.append(vp)
        ss_list.append(ss); ks_list.append(kss); vs_list.append(vss)
    state_gla_prompt = jnp.stack(sp_list)
    cache_swa_k_prompt = jnp.stack(kp_list)
    cache_swa_v_prompt = jnp.stack(vp_list)
    state_gla_sample = jnp.stack(ss_list)
    cache_swa_k_sample = jnp.stack(ks_list)
    cache_swa_v_sample = jnp.stack(vs_list)
    return (yp, ys, state_gla_prompt, cache_swa_k_prompt, cache_swa_v_prompt,
            state_gla_sample, cache_swa_k_sample, cache_swa_v_sample)


_drawn_inputs = setup_inputs


def setup_inputs(seed=0):
    import zlib

    import numpy as np

    out = dict(_drawn_inputs(seed))
    spreads = {}
    factors = {'swa_sinks': 8.0}
    for name, (base, spread) in spreads.items():
        noise = np.random.default_rng([zlib.crc32(name.encode()), seed]).standard_normal(out[name].shape)
        drawn = base * np.exp(spread * noise) if base else spread * noise
        out[name] = __import__('jax').numpy.asarray(drawn.astype(out[name].dtype))
    for name, factor in factors.items():
        out[name] = (out[name] * factor).astype(out[name].dtype)
    return out
```

```python
from contextlib import ExitStack

import concourse.bass as bass
from concourse import mybir

F32 = mybir.dt.float32
F16 = mybir.dt.float16
ALU = mybir.AluOpType
ACT = mybir.ActivationFunctionType
AX_X = mybir.AxisListType.X

P = 128
D = 1024
KC = D // P
SEQ, DEC_SEQ, PAST = 4096, 64, 1024
CHUNK = 64
NT = SEQ // P
LOOP_END = NT - 2
EPS = 1e-6
GH, DK, DV = 4, 64, 128
LOWRANK = 16
TAU = 16.0
HEADS, KVH, HD = 8, 2, 64
ROPE_HALF = HD // 8
GROUPS = 8
WSCALE = 64.0
DESCALE = 1.0 / WSCALE
MID0, MID1 = 32, 96

C_GQ, C_GK, C_GV, C_GG, C_GA, C_SQ, C_SK, C_SV, C_SG, C_END = (
    0, 256, 512, 1024, 1536, 1552, 2064, 2192, 2320, 2832)
W_QK, W_KSG, W_SQ, W_V, W_GG, W_SG = 0, 512, 784, 1296, 1808, 2320
KSG = 272
UNIT = 256
IN_UNITS = [(W_QK, C_GQ, 256), (W_QK + 256, C_GK, 256),
            (W_KSG, C_SK, 256), (W_KSG + 256, C_GA, 16),
            (W_SQ, C_SQ, 256), (W_SQ + 256, C_SQ + 256, 256),
            (W_V, C_GV, 256), (W_V + 256, C_GV + 256, 256),
            (W_GG, C_GG, 256), (W_GG + 256, C_GG + 256, 256),
            (W_SG, C_SG, 256), (W_SG + 256, C_SG + 256, 256)]
ADA_UNITS = 3 * D // UNIT
OUT_UNITS = D // UNIT
UNITS = [("ada", i, i % 3) for i in range(ADA_UNITS)]
UNITS += [("in", i, i % 2) for i in range(len(IN_UNITS))] + [("out", i, i % 2) for i in range(OUT_UNITS)]


def slot_use(n):
    return sum(1 for u in UNITS[:n] if u[2] == UNITS[n][2])


def unit_number(kind, i):
    return [u[:2] for u in UNITS].index((kind, i))


class Tile:

    def __init__(self, t, half, par):
        peeled = isinstance(t, int)
        self.t, self.half, self.par = t, half, par
        self.prev = not (peeled and t == 0)
        self.cur = not (peeled and t == NT + 1)
        self.next = not (peeled and t >= NT)
        self.first = peeled and t == 0
        self.second = peeled and t == 1
        self.last = peeled and t == NT - 1
        self.sample = peeled and t == NT
        self.after = peeled and t == NT + 1


def hybrid_layer(nc, x_prompt, x_sample, c_prompt, c_sample, state_gla, cache_k, cache_v, w_ada, b_ada, g_pre,
                 g_post, w_in, w_alpha, b_alpha, gla_norm_g, swa_sinks, w_out, trig,
                 y_prompt, y_sample, st_prompt, k_prompt, v_prompt, st_sample, k_sample, v_sample):
    ctx = ExitStack()
    with ctx:
        ctx.enter_context(nc.allow_non_contiguous_dma(reason="small column vectors, once"))

        def sb(name, shape, dt=F32):
            return ctx.enter_context(nc.sbuf_tensor(name, shape, dt))

        def psum(name, shape):
            return ctx.enter_context(nc.psum_tensor(name, shape, F32))

        w_hi = sb("w_hi", [P, KC, C_END], F16)
        w_lo = sb("w_lo", [P, KC, C_END], F16)
        wo_hi = sb("wo_hi", [P, KC, D], F16)
        wo_lo = sb("wo_lo", [P, KC, D], F16)
        stage = sb("stage", [P, 4 * D])
        late = sb("late", [P, 2 * D])
        slots = [stage[:, 0:2 * D], stage[:, 2 * D:4 * D], late[:, :]]
        gate_row = stage[:, 0:D]
        y_buf = [stage[:, 2 * D:3 * D], stage[:, 3 * D:4 * D]]
        gate_diag = y_buf[0].rearrange("p (c k) -> p c k", c=KC)
        probs = late[:, 0:D].rearrange("p (g k) -> p g k", g=GROUPS)
        probsT = late[:, D:2 * D].rearrange("p (g k) -> p g k", g=GROUPS)
        mixT = late[:, D:2 * D].bitcast(F16).rearrange("p (s c k) -> p s c k", s=2, c=KC)
        x_in = sb("x_in", [P, 2, D])
        x_res = sb("x_res", [P, D])
        trig_in = sb("trig_in", [P, 2, 2 * ROPE_HALF])
        xs = sb("xs", [P, D])
        h_ch = xs[:, :].rearrange("p (c k) -> p c k", c=KC)
        hT = sb("hT", [P, 2, 2, KC, P], F16)
        v_tok = sb("v_tok", [P, GH * DV])
        qk_tok = sb("qk_tok", [P, 5, P])
        ga_tok = sb("ga_tok", [P, LOWRANK])
        rope_cos = sb("rope_cos", [P, 10, 2, ROPE_HALF])
        rope_sin = sb("rope_sin", [P, 10, 2, ROPE_HALF])
        qT = sb("qT", [P, 2, 4, CHUNK])
        kA = sb("kA", [P, 2, P])
        kA_s = sb("kA_s", [P, P])
        kB = sb("kB", [P, P])
        vA = sb("vA", [P, 2, P])
        vA_s = sb("vA_s", [P, P])
        vB = sb("vB", [P, 2, P])
        gates = sb("gates", [P, D])
        etmp = sb("etmp", [P, 512])
        lsp = sb("lsp", [P, 2, P])
        la = sb("la", [P, 2, P])
        bsum = sb("bsum", [P, 2, P])
        q_d = sb("q_d", [P, 2, P])
        k_d = sb("k_d", [P, 2, P])
        q_int, k_out = lsp, la
        k_off = sb("k_off", [P, 2, CHUNK])
        k_tok = sb("k_tok", [P, 2, P])
        aT = sb("aT", [P, 2, 2, P])
        S = sb("S", [P, 2, 2, DV])
        S_s = sb("S_s", [P, 2, 2, DV])
        fac_in = sb("fac_in", [P, 2, 6])
        fac = sb("fac", [P, 2, 6])
        ident = sb("ident", [P, P])
        causal = sb("causal", [P, P])
        scan_mask = sb("scan_mask", [P, 2 * P])
        gnorm = sb("gnorm", [P, DV])
        w_al = sb("w_al", [LOWRANK + 1, GH * DK])
        gaT = sb("gaT", [32, P])
        cache_k_tok = sb("cache_k_tok", [CHUNK, P])
        sinks = sb("sinks", [P, GROUPS])
        c_col = sb("c_col", [P, KC, 2])
        c_tmp = sb("c_tmp", [P, KC, 2])
        c_silu = sb("c_silu", [P, KC, 2])
        b_col = sb("b_col", [P, 3 * KC])
        g_col = sb("g_col", [P, 2, KC])
        mod = sb("mod", [P, 3 * KC, 2])
        x_ss = sb("x_ss", [P, 2])
        x_ln = sb("x_ln", [P, 1])
        x_r = sb("x_r", [P, 2])
        o_ss = sb("o_ss", [P, 4])
        o_ln = sb("o_ln", [P, 4])
        o_r = sb("o_r", [P, 4])
        y_ss = sb("y_ss", [P, 1])
        y_ln = sb("y_ln", [P, 1])
        y_r = sb("y_r", [P, 1])
        smax = sb("smax", [P, GROUPS])
        m_pos = sb("m_pos", [P, GROUPS])
        m_neg = sb("m_neg", [P, GROUPS])
        sink_d = sb("sink_d", [P, GROUPS])
        sink_e = sb("sink_e", [P, GROUPS])
        row_sum = sb("row_sum", [P, GROUPS])
        den = sb("den", [P, GROUPS])
        rden = sb("rden", [P, GROUPS])
        junk = sb("junk", [P, GH * DV], F16)
        eps = sb("eps", [P, 1])
        ln_scale = sb("ln_scale", [P, 1])

        pairP = psum("pairP", [P, 2 * 512])
        pairQ = psum("pairQ", [P, 2 * 512])
        bank4 = psum("bank4", [P, 512])
        bank5 = psum("bank5", [P, 512])
        bank6 = psum("bank6", [P, 512])
        bank7 = psum("bank7", [P, 512])
        pairP_c = pairP[:, :].rearrange("p (c k) -> p c k", c=KC)
        scores = pairQ[:, :].rearrange("p (g k) -> p g k", g=GROUPS)
        qk_ch = bank4[:, :].rearrange("p (b k) -> p b k", b=4)
        z_ch = bank5[:, 0:256].rearrange("p (b k) -> p b k", b=2)
        a_ps = [bank5[:, 0:256].rearrange("p (b k) -> p b k", b=2), bank4[:, 0:256].rearrange("p (b k) -> p b k", b=2)]
        kt_ps = bank4[:, 256:512].rearrange("p (b k) -> p b k", b=2)
        u_ps = bank5[:, 256:512].rearrange("p (b k) -> p b k", b=2)
        mod_ps = pairQ[:, 0:6 * KC].rearrange("p (b c) -> p b c", c=2)

        sem = {}
        for name in ("const_load c_silu_d c_exp c_one c_rec c_silu eps_set ident_z ident mask_z causal scan_z scan_m "
                     "ss_zero gaT_one sinks mod_done mod_sum mod_out zeroed kcache_t cache_kA gdiag_d gate_bc gate_row "
                     "x_sq x_lnd x_rs xs h_f32 h_hi h_lo res_copied y_final out_stored qk_mm ksg_mm pv_mm sq_mm gat_mm "
                     "mixt_mm v_mm z_mm qks_mm out_mm sc_mm gg_mm xt_mm a_mm sg_mm o_mm u_mm pt_mm ksg_ev sq_ev gat_ev "
                     "pt_ev mixt_hi mixt_lo v_ev qks_ev rope_m rope_s rope va_prev z_abs z_e z_l la_d scan bc_d fac_d "
                     "fac_e e_pos e_neg qk_d k_off gla_sc at_d kt_ev s_upd o_sq o_lnd o_rs mix_gla mix_swa smax m_pos "
                     "m_neg sink_d sink_e p_exp den rden probs gg_e gg_1 gg_r gg_x gg_g sg_e sg_1 sg_r sg_g y_sq y_lnd "
                     "y_rs y_mul").split():
            sem[name] = ctx.enter_context(nc.semaphore(name))
        staged = [ctx.enter_context(nc.semaphore(f"staged{i}")) for i in range(3)]
        slot_free = [ctx.enter_context(nc.semaphore(f"slot_free{i}")) for i in range(3)]
        x_loaded = [ctx.enter_context(nc.semaphore(f"x_loaded{i}")) for i in range(2)]
        y_stored = [ctx.enter_context(nc.semaphore(f"y_stored{i}")) for i in range(2)]
        w_split = ctx.enter_context(nc.semaphore("w_split"))
        w_half = ctx.enter_context(nc.semaphore("w_half"))

        def all_tiles(eng, program, peel):
            for t in range(peel):
                program(Tile(t, t // 2, t % 2))
            with eng.Fori(peel // 2, LOOP_END // 2) as k:
                program(Tile(k * 2, k, 0))
                program(Tile(k * 2 + 1, k, 1))
            for t in range(LOOP_END, NT + 2):
                program(Tile(t, t // 2, t % 2))

        in_units_before = {W_KSG: 4, W_SQ: 6, W_V: 8, W_GG: 10, W_SG: 12}
        block = ctx.enter_context(nc.Block())

        @block.sync
        def _(sp):
            def load_x(t, par):
                if isinstance(t, int) and t == NT:
                    sp.dma_start(x_in[0:DEC_SEQ, par, :], x_sample[0]).then_inc(x_loaded[par], 16)
                else:
                    sp.dma_start(x_in[:, par, :], x_prompt[0, bass.ds(t * P, P), :]).then_inc(x_loaded[par], 16)
                sp.dma_start(trig_in[:, par, :], trig[bass.ds(t * P, P), :]).then_inc(x_loaded[par], 16)

            load_x(0, 0)
            for n, (kind, i, slot) in enumerate(UNITS):
                before = [m for m in range(n) if UNITS[m][2] == slot]
                if before and before[-1] < ADA_UNITS:
                    sp.wait_ge(slot_free[slot], len(before))
                elif before:
                    sp.wait_ge(w_split, before[-1] - ADA_UNITS + 1)
                if kind == "ada":
                    src, w = w_ada[0, :, i * UNIT:(i + 1) * UNIT], UNIT
                elif kind == "in":
                    src, w = w_in[0, :, IN_UNITS[i][1]:IN_UNITS[i][1] + IN_UNITS[i][2]], IN_UNITS[i][2]
                else:
                    src, w = w_out[0, :, i * UNIT:(i + 1) * UNIT], UNIT
                dst = slots[slot][:, 0:KC * w].rearrange("p (c n) -> p c n", c=KC)
                sp.dma_start(dst, src.rearrange("(c p) n -> p c n", p=P)).then_inc(staged[slot], 16)
                if n == ADA_UNITS:
                    load_x(1, 1)
            sp.dma_start(k_sample[0, 0, 0:CHUNK], cache_k[0, 0, CHUNK:2 * CHUNK]).then_inc(sem["out_stored"], 16)
            sp.dma_start(v_sample[0, 0, 0:CHUNK], cache_v[0, 0, CHUNK:2 * CHUNK]).then_inc(sem["out_stored"], 16)

            def program(c):
                if c.prev:
                    sp.wait_ge(sem["y_final"], c.t)
                    src = y_buf[1 - c.par]
                    if c.after:
                        sp.dma_start(y_sample[0], src[0:DEC_SEQ, :]).then_inc(y_stored[1 - c.par], 16)
                    else:
                        sp.dma_start(y_prompt[0, bass.ds((c.t - 1) * P, P), :], src).then_inc(y_stored[1 - c.par], 16)
                if c.cur:
                    sp.wait_ge(x_loaded[c.par], 32 * (c.half + 1))
                    sp.dma_start(x_res[:, :], x_in[:, c.par, :]).then_inc(sem["res_copied"], 16)
                if not isinstance(c.t, int) or c.t + 2 <= NT:
                    sp.wait_ge(sem["res_copied"], 16 * (c.t + 1))
                    sp.wait_ge(sem["xs"], c.t + 1)
                    sp.wait_ge(sem["rope"], c.t + 1)
                    load_x(c.t + 2, c.par)
                if c.last or c.sample:
                    n = P if c.last else DEC_SEQ
                    ko, vo = (k_prompt[0, 0], v_prompt[0, 0]) if c.last else (
                        k_sample[0, 0, CHUNK:], v_sample[0, 0, CHUNK:])
                    sp.wait_ge(sem["rope"], c.t + 1)
                    sp.wait_ge(sem["ksg_ev"], c.t + 1)
                    sp.dma_start(ko.rearrange("t h d -> t (h d)"), qk_tok[0:n, 4, :]).then_inc(sem["out_stored"], 16)
                    sp.dma_start(vo.rearrange("t h d -> t (h d)"), vB[0:n, c.par, :]).then_inc(sem["out_stored"], 16)
                if c.sample or c.after:
                    st, buf = (st_prompt, S) if c.sample else (st_sample, S_s)
                    sp.wait_ge(sem["s_upd"], c.t)
                    for q in range(2):
                        sp.dma_start(st[0, 0].rearrange("(b q) k v -> q k b v", q=2)[q],
                                     buf[DK * q:DK * q + DK, :, q, :]).then_inc(sem["out_stored"], 16)

            all_tiles(sp, program, 2)
            sp.wait_ge(sem["out_stored"], 16 * 10)
            sp.wait_ge(y_stored[0], 16 * (NT // 2 + 1))
            sp.wait_ge(y_stored[1], 16 * (NT // 2))

        @block.tensor
        def _(pe):
            def split_product(out, a, b):
                for c in range(KC):
                    for n, (i, j) in enumerate(((0, 0), (0, 1), (1, 0))):
                        last = pe.matmul(out, a(c, i), b(c, j), start=(c == 0 and n == 0),
                                         stop=(c == KC - 1 and n == 2))
                return last

            pe.wait_ge(sem["c_silu"], 1)
            for n in range(ADA_UNITS):
                slot = UNITS[n][2]
                pe.wait_ge(staged[slot], 16 * (slot_use(n) + 1))
                w = slots[slot].rearrange("p (c n) -> p c n", c=KC)
                for j in range(UNIT // P):
                    for c in range(KC):
                        last = pe.matmul(mod_ps[:, n * (UNIT // P) + j, :], w[:, c, j * P:(j + 1) * P], c_silu[:, c, :],
                                         start=(c == 0), stop=(c == KC - 1))
                last.then_inc(slot_free[slot], 1)
            pe.wait_ge(sem["const_load"], 16 * 18)
            pe.wait_ge(sem["ident"], 1)
            pe.transpose(bank4[:, 0:CHUNK], cache_k_tok[:, :], ident[0:CHUNK, 0:CHUNK]).then_inc(sem["kcache_t"], 1)
            pe.wait_ge(sem["scan_m"], 2)
            pe.wait_ge(sem["xs"], 1)
            for c in range(KC):
                last = pe.transpose(pairP_c[:, c, :], xs[:, c * P:(c + 1) * P], ident[:, :])
            last.then_inc(sem["xt_mm"], 1)

            def program(c):
                t, par = c.t, c.par

                def h(cc, i):
                    return hT[:, par, i, cc, :]

                def project(bank, width, col, done):
                    if c.first:
                        pe.wait_ge(w_split, in_units_before[col])
                    split_product(bank[:, 0:width], h,
                                  lambda cc, i: (w_hi, w_lo)[i][:, cc, col:col + width]).then_inc(done, 1)

                if c.cur:
                    pe.wait_ge(sem["h_lo"], t + 1)
                    if c.first:
                        pe.wait_ge(w_split, 2)
                        pe.wait_ge(sem["cache_kA"], 1)
                    else:
                        pe.wait_ge(sem["at_d"], t)
                    for b in range(4):
                        last = split_product(qk_ch[:, b, :],
                                             lambda cc, i: (w_hi, w_lo)[i][:, cc, W_QK + b * P:W_QK + (b + 1) * P], h)
                    last.then_inc(sem["qk_mm"], 1)
                if c.prev:
                    pe.wait_ge(sem["probs"], t)
                    if c.after:
                        pe.wait_ge(sem["y_mul"], t - 1)
                    else:
                        pe.wait_ge(sem["h_f32"], t + 1)
                    for g in range(GROUPS):
                        last = pe.transpose(pairP_c[:, g, :], probs[:, g, :], ident[:, :])
                    last.then_inc(sem["pt_mm"], 1)
                if c.cur:
                    if c.prev:
                        pe.wait_ge(sem["s_upd"], t)
                    project(bank5, KSG, W_KSG, sem["ksg_mm"])
                if c.prev:
                    pe.wait_ge(sem["pt_ev"], t)
                    pe.wait_ge(sem["sg_g"], t)
                    pe.wait_ge(sem["va_prev"], t)
                    for ch in range(2):
                        vsrc = vB[:, 1 - par, :] if ch else (vA_s[:, :] if c.after else vA[:, 1 - par, :])
                        for head in range(HEADS):
                            g, pp, e = head // 4, head % 4 // 2, head % 2
                            last = pe.matmul(bank6[CHUNK * ch:CHUNK * (ch + 1), head * HD:(head + 1) * HD],
                                             probsT[:, 4 * g + 2 * ch + pp, CHUNK * e:CHUNK * (e + 1)],
                                             vsrc[:, HD * g:HD * (g + 1)], start=True, stop=True)
                    last.then_inc(sem["pv_mm"], 1)
                if c.cur:
                    if c.prev:
                        pe.wait_ge(sem["mix_gla"], t)
                    project(bank7, 512, W_SQ, sem["sq_mm"])
                    pe.wait_ge(sem["ksg_ev"], t + 1)
                    pe.transpose(bank5[0:LOWRANK, 0:P], ga_tok[:, :], ident[:, :]).then_inc(sem["gat_mm"], 1)
                if c.second or c.after:
                    pe.wait_ge(sem["gdiag_d"], 1 if c.second else 2)
                    for n in range(2):
                        last = pe.matmul(pairP[:, 512 * n:512 * (n + 1)],
                                         scan_mask[:, 1:2].to_broadcast([P, P]),
                                         gate_diag[:, 4 * n:4 * n + 4, :], start=True, stop=True)
                    last.then_inc(sem["gate_bc"], 1)
                    pe.wait_ge(sem["gate_row"], 1 if c.second else 2)
                if c.prev:
                    pe.wait_ge(sem["mix_swa"], t)
                    pe.wait_ge(sem["mix_gla"], t)
                    for cc in range(KC):
                        last = pe.transpose(pairP_c[:, cc, :], gates[:, cc * P:(cc + 1) * P], ident[:, :])
                    last.then_inc(sem["mixt_mm"], 1)
                if c.cur:
                    project(bank6, 512, W_V, sem["v_mm"])
                    pe.wait_ge(sem["gat_ev"], t + 1)
                    for b in range(2):
                        last = pe.matmul(z_ch[:, b, :], w_al[:, b * P:(b + 1) * P], gaT[0:LOWRANK + 1, :],
                                         start=True, stop=True)
                    last.then_inc(sem["z_mm"], 1)
                    pe.wait_ge(sem["rope"], t + 1)
                    if c.prev:
                        pe.wait_ge(sem["p_exp"], t)
                    for b in range(5):
                        last = pe.transpose(pairQ[:, b * P:(b + 1) * P], qk_tok[:, b, :], ident[:, :])
                    last.then_inc(sem["qks_mm"], 1)
                if c.prev:
                    pe.wait_ge(sem["mixt_lo"], t)
                    if c.second:
                        pe.wait_ge(w_split, len(IN_UNITS) + OUT_UNITS)
                    for n in range(2):
                        last = split_product(pairP[:, 512 * n:512 * (n + 1)], lambda cc, i: mixT[:, i, cc, :],
                                             lambda cc, i: (wo_hi, wo_lo)[i][:, cc, 512 * n:512 * (n + 1)])
                    last.then_inc(sem["out_mm"], 1)
                if not c.cur:
                    return
                pe.wait_ge(sem["qks_ev"], t + 1)
                for ch in range(2):
                    for pp in range(2):
                        for g in range(KVH):
                            kk = kB[:, :] if ch else (kA_s[:, :] if c.sample else kA[:, par, :])
                            last = pe.matmul(scores[:, 4 * g + 2 * ch + pp, :],
                                             qT[HD * g:HD * (g + 1), ch, 2 * pp:2 * pp + 2, :],
                                             kk[HD * g:HD * (g + 1), :], start=True, stop=True)
                last.then_inc(sem["sc_mm"], 1)
                pe.wait_ge(sem["sq_ev"], t + 1)
                project(bank7, 512, W_GG, sem["gg_mm"])
                if c.next:
                    pe.wait_ge(sem["xs"], t + 2)
                    if c.prev:
                        pe.wait_ge(sem["y_mul"], t)
                    for cc in range(KC):
                        last = pe.transpose(pairP_c[:, cc, :], xs[:, cc * P:(cc + 1) * P], ident[:, :])
                    last.then_inc(sem["xt_mm"], 1)
                pe.wait_ge(sem["gla_sc"], t + 1)
                for b in range(2):
                    pe.transpose(kt_ps[:, b, :], k_out[:, b, :], ident[:, :])
                for b in range(2):
                    for q in range(2):
                        r = slice(DK * q, DK * (q + 1))
                        pe.matmul(a_ps[q][0:64, b, 0:64], k_d[r, b, 0:64], q_d[r, b, 0:64], start=True, stop=True)
                        pe.matmul(a_ps[q][0:64, b, 64:128], k_off[r, b, :], q_d[r, b, 64:128], start=True, stop=True)
                        last = pe.matmul(a_ps[q][64:128, b, 64:128], k_d[r, b, 64:128], q_d[r, b, 64:128],
                                         start=True, stop=True)
                last.then_inc(sem["a_mm"], 1)
                pe.wait_ge(sem["v_ev"], t + 1)
                project(bank6, 512, W_SG, sem["sg_mm"])
                pe.wait_ge(sem["at_d"], t + 1)
                pe.wait_ge(sem["gg_x"], t + 1)
                if c.prev:
                    pe.wait_ge(sem["s_upd"], t)
                st = S_s if c.sample else S
                for b in range(2):
                    pe.matmul(bank7[:, 2 * b * DV:2 * (b + 1) * DV], q_int[:, b, :], st[:, b, :, :],
                              start=True, stop=False)
                    for q in range(2):
                        o = slice((2 * b + q) * DV, (2 * b + q + 1) * DV)
                        last = pe.matmul(bank7[:, o], aT[:, b, q, :], v_tok[:, o], start=False, stop=(q == 1))
                last.then_inc(sem["o_mm"], 1)
                n = DEC_SEQ if c.sample else P
                for hd in range(GH):
                    b, q = hd // 2, hd % 2
                    last = pe.matmul(u_ps[DK * q:DK * (q + 1), b, :], k_tok[0:n, b, DK * q:DK * (q + 1)],
                                     v_tok[0:n, hd * DV:(hd + 1) * DV], start=True, stop=True)
                last.then_inc(sem["u_mm"], 1)

            all_tiles(pe, program, 2)

        @block.scalar
        def _(act):
            act.preload_act_table_set("natural_log_exp_and_others")

            def small(dst, src):
                act.dma_start(dst, src).then_inc(sem["const_load"], 16)

            for i, cvec in enumerate((c_prompt, c_sample)):
                small(c_col[:, :, i], cvec.rearrange("o (c p) -> p (o c)", p=P))
            act.wait_ge(sem["const_load"], 32)
            act.activation(c_tmp[:, :, :], c_col[:, :, :], ACT.Exp, scale=-1.0).then_inc(sem["c_exp"], 1)
            small(b_col[:, :], b_ada.rearrange("o (c p) -> p (o c)", p=P))
            for i, g in enumerate((g_pre, g_post)):
                small(g_col[:, i, :], g.rearrange("o (c p) -> p (o c)", p=P))
            small(gnorm[:, :], gla_norm_g[0].partition_broadcast(P))
            small(w_al[0:LOWRANK, :], w_alpha[0])
            small(w_al[LOWRANK:LOWRANK + 1, :], b_alpha)
            act.wait_ge(sem["ss_zero"], 1)
            small(cache_k_tok[:, :], cache_k[0, 0, CHUNK:2 * CHUNK].rearrange("t h d -> t (h d)"))
            small(vA_s[CHUNK:P, :], cache_v[0, 0, CHUNK:2 * CHUNK].rearrange("t h d -> t (h d)"))
            for q in range(2):
                small(S_s[DK * q:DK * q + DK, :, q, :],
                      state_gla[0, 0].rearrange("(b q) k v -> q k b v", q=2)[q])
            sink_v = swa_sinks[0].rearrange("(g pp e) -> e g pp", g=KVH, pp=2)
            sink_d4 = sinks[:, :].rearrange("p (g c pp) -> p g c pp", g=KVH, c=2)
            for e in range(2):
                for g in range(KVH):
                    small(sink_d4[CHUNK * e:CHUNK * (e + 1), g, 0, :], sink_v[e, g].partition_broadcast(CHUNK))
            act.wait_ge(sem["const_load"], 16 * 16)
            for e in range(2):
                act.dma_start(sink_d4[CHUNK * e:CHUNK * (e + 1), :, 1, :],
                              sink_d4[CHUNK * e:CHUNK * (e + 1), :, 0, :]).then_inc(sem["const_load"], 16)

            def rsqrt_of(dst, tmp, ssum, n, ln_done, done, count, scale_out=None):
                act.activation(tmp, ssum, ACT.Ln, bias=eps[:, :], scale=1.0 / n).then_inc(ln_done, 1)
                act.wait_ge(ln_done, count)
                if scale_out is None:
                    act.activation(dst, tmp, ACT.Exp, scale=-0.5).then_inc(done, 1)
                else:
                    act.activation(dst, tmp, ACT.Exp, bias=scale_out, scale=-0.5).then_inc(done, 1)

            def x_stats(t, half, par):
                act.wait_ge(x_loaded[par], 32 * (half + 1))
                if not isinstance(t, int) or t >= 2:
                    act.wait_ge(sem["sg_mm"], t - 1)
                    act.wait_ge(sem["xs"], t - 1)
                act.activation(hT[:, par, 0, :, :], x_in[:, par, :].rearrange("p (c k) -> p c k", c=KC), ACT.Square,
                               accum_out=x_ss[:, par:par + 1]).then_inc(sem["x_sq"], 1)
                act.wait_ge(sem["x_sq"], t + 1)
                rsqrt_of(x_r[:, par:par + 1], x_ln[:, :], x_ss[:, par:par + 1], D, sem["x_lnd"], sem["x_rs"], t + 1)

            def split_hi(units):
                for kind, i in units:
                    n = unit_number(kind, i)
                    slot = UNITS[n][2]
                    col, _, w = IN_UNITS[i] if kind == "in" else (i * UNIT, 0, UNIT)
                    act.wait_ge(staged[slot], 16 * (slot_use(n) + 1))
                    act.activation((w_hi if kind == "in" else wo_hi)[:, :, col:col + w],
                                   slots[slot][:, 0:KC * w].rearrange("p (c n) -> p c n", c=KC),
                                   ACT.Copy, scale=WSCALE).then_inc(w_half, 1)

            act.wait_ge(sem["eps_set"], 2)
            x_stats(0, 0, 0)

            def h_hi(t, par):
                act.wait_ge(sem["h_f32"], t + 1)
                act.activation(hT[:, par, 0, :, :], h_ch, ACT.Copy).then_inc(sem["h_hi"], 1)

            h_hi(0, 0)
            split_hi([("in", i) for i in range(4)])

            def program(c):
                t, par = c.t, c.par
                if c.prev:
                    act.wait_ge(sem["o_mm"], t)
                    for hd in range(GH):
                        last = act.activation(junk[:, hd * DV:(hd + 1) * DV], bank7[:, hd * DV:(hd + 1) * DV], ACT.Square,
                                              accum_out=o_ss[:, hd:hd + 1])
                    last.then_inc(sem["o_sq"], 1)
                    act.wait_ge(sem["o_sq"], t)
                    rsqrt_of(o_r[:, :], o_ln[:, :], o_ss[:, :], DV, sem["o_lnd"], sem["o_rs"], t)
                    act.wait_ge(sem["pt_mm"], t)
                    act.activation(probsT, pairP_c, ACT.Copy).then_inc(sem["pt_ev"], 1)
                if c.cur:
                    if c.first:
                        split_hi([("in", 4), ("in", 5), ("in", 6), ("in", 7)])
                    act.wait_ge(sem["ksg_mm"], t + 1)
                    if c.prev:
                        act.wait_ge(sem["qks_mm"], t)
                    if c.sample:
                        act.wait_ge(sem["out_stored"], 16 * 4)
                    act.activation(ga_tok[:, :], bank5[:, 256:KSG], ACT.Copy, scale=DESCALE)
                    act.activation(qk_tok[:, 4, :], bank5[:, 0:P], ACT.Copy, scale=DESCALE)
                    va = vA_s[0:CHUNK, :] if c.sample else vA[0:CHUNK, par, :]
                    act.activation(va, bank5[0:CHUNK, P:2 * P], ACT.Copy, scale=DESCALE)
                    act.activation(vB[:, par, :], bank5[:, P:2 * P], ACT.Copy, scale=DESCALE).then_inc(sem["ksg_ev"], 1)
                    act.wait_ge(sem["sq_mm"], t + 1)
                    act.activation(qk_tok[:, 0:4, :].rearrange("p b (g k) -> p b g k", g=KVH),
                                   bank7[:, :].rearrange("p (g b k) -> p b g k", g=KVH, b=4),
                                   ACT.Copy, scale=DESCALE).then_inc(sem["sq_ev"], 1)
                    if c.prev:
                        act.wait_ge(sem["pv_mm"], t)
                    act.wait_ge(sem["ksg_ev"], t + 1)
                    act.activation(vA[CHUNK:P, 1 - par, :], vB[CHUNK:P, par, :], ACT.Copy).then_inc(sem["va_prev"], 1)
                    act.wait_ge(sem["gat_mm"], t + 1)
                    if c.first:
                        act.wait_ge(sem["gaT_one"], 1)
                    act.activation(gaT[0:LOWRANK, :], bank5[0:LOWRANK, 0:P], ACT.Copy).then_inc(sem["gat_ev"], 1)
                    if c.first:
                        split_hi([("in", 8), ("in", 9)])
                if c.second or c.after:
                    act.wait_ge(sem["gate_bc"], 1 if c.second else 2)
                    act.activation(gate_row, pairP[:, :], ACT.Copy).then_inc(sem["gate_row"], 1)
                if c.prev:
                    act.wait_ge(sem["mixt_mm"], t)
                    act.activation(mixT[:, 0, :, :], pairP_c, ACT.Copy).then_inc(sem["mixt_hi"], 1)
                if c.cur:
                    act.wait_ge(sem["v_mm"], t + 1)
                    if c.prev:
                        act.wait_ge(sem["u_mm"], t)
                    act.activation(v_tok[:, :], bank6[:, :], ACT.Copy, scale=DESCALE).then_inc(sem["v_ev"], 1)
                    if c.first:
                        split_hi([("in", 10), ("in", 11)])
                    act.wait_ge(sem["z_mm"], t + 1)
                    if c.prev:
                        act.wait_ge(sem["o_mm"], t)
                    act.activation(lsp[:, :, :], z_ch, ACT.Abs).then_inc(sem["z_abs"], 1)
                    act.wait_ge(sem["z_abs"], t + 1)
                    act.activation(lsp[:, :, :], lsp[:, :, :], ACT.Exp, scale=-1.0).then_inc(sem["z_e"], 1)
                    act.wait_ge(sem["z_e"], t + 1)
                    act.activation(lsp[:, :, :], lsp[:, :, :], ACT.Ln, bias=1.0).then_inc(sem["z_l"], 1)
                if c.next:
                    x_stats(t + 1, c.half + par, 1 - par)
                if c.cur:
                    act.wait_ge(sem["bc_d"], t + 1)
                    if c.prev:
                        act.wait_ge(sem["a_mm"], t)
                    act.activation(k_d[:, :, :], q_d[:, :, :], ACT.Exp, scale=-1.0 / TAU).then_inc(sem["e_neg"], 1)
                    act.wait_ge(sem["e_neg"], t + 1)
                    act.activation(q_d[:, :, :], q_d[:, :, :], ACT.Exp, scale=1.0 / TAU).then_inc(sem["e_pos"], 1)
                    act.wait_ge(sem["fac_d"], t + 1)
                    act.activation(fac[:, :, :], fac_in[:, :, :], ACT.Exp, scale=1.0 / TAU).then_inc(sem["fac_e"], 1)
                if c.prev:
                    act.wait_ge(sem["out_mm"], t)
                    if not isinstance(t, int) or t >= 3:
                        act.wait_ge(y_stored[1 - par], 16 * (c.half - (1 - par)))
                    act.activation(y_buf[1 - par], pairP[:, :], ACT.Square, accum_out=y_ss[:, :]).then_inc(sem["y_sq"], 1)
                    act.wait_ge(sem["y_sq"], t)
                    rsqrt_of(y_r[:, :], y_ln[:, :], y_ss[:, :], D * WSCALE * WSCALE, sem["y_lnd"], sem["y_rs"], t, ln_scale[:, :])
                if not c.cur:
                    return
                if c.first:
                    split_hi([("out", i) for i in range(OUT_UNITS)])
                act.wait_ge(sem["m_neg"], t + 1)
                if c.prev:
                    act.wait_ge(sem["pt_mm"], t)
                if c.first:
                    act.wait_ge(sem["zeroed"], 1)
                for g in range(GROUPS):
                    w = CHUNK if c.first and g % 4 < 2 else P
                    act.activation(probs[:, g, 0:w], scores[:, g, 0:w], ACT.Exp, bias=m_neg[:, g:g + 1],
                                   scale=HD ** -0.5, accum_out=row_sum[:, g:g + 1])
                act.wait_ge(sem["sink_d"], t + 1)
                act.activation(sink_e[:, :], sink_d[:, :], ACT.Exp).then_inc(sem["p_exp"], 1)
                act.wait_ge(sem["gg_mm"], t + 1)
                if c.prev:
                    act.wait_ge(sem["sg_g"], t)
                act.activation(etmp[:, :], bank7[:, :], ACT.Exp, scale=-DESCALE).then_inc(sem["gg_e"], 1)
                if c.next:
                    h_hi(t + 1, 1 - par)
                act.wait_ge(sem["sg_mm"], t + 1)
                act.wait_ge(sem["gg_x"], t + 1)
                act.activation(etmp[:, :], bank6[:, :], ACT.Exp, scale=-DESCALE).then_inc(sem["sg_e"], 1)

            all_tiles(act, program, 4)

        @block.vector
        def _(dve):
            dve.memset(eps[:, :], EPS).then_inc(sem["eps_set"], 1)
            dve.memset(ln_scale[:, :], -4.1588830833596715).then_inc(sem["eps_set"], 1)
            dve.memset(S_s[:, :, :, :], 0.0).then_inc(sem["ss_zero"], 1)
            dve.memset(vA[CHUNK:P, 0, :], 0.0)
            dve.memset(gaT[:, :], 1.0).then_inc(sem["gaT_one"], 1)
            dve.wait_ge(sem["c_exp"], 1)
            dve.tensor_scalar(c_tmp[:, :, :], c_tmp[:, :, :], 1.0, None, ALU.add).then_inc(sem["c_one"], 1)
            dve.wait_ge(sem["c_one"], 1)
            dve.reciprocal(c_tmp[:, :, :], c_tmp[:, :, :]).then_inc(sem["c_rec"], 1)
            dve.wait_ge(sem["c_rec"], 1)
            dve.tensor_tensor(c_silu[:, :, :], c_tmp[:, :, :], c_col[:, :, :], ALU.mult).then_inc(sem["c_silu"], 1)
            dve.wait_ge(sem["const_load"], 16 * 18)
            for i in range(3):
                dve.wait_ge(slot_free[i], ADA_UNITS // 3)
            dve.tensor_tensor(mod[:, :, :], mod_ps, b_col[:, :].unsqueeze(2).to_broadcast([P, 3 * KC, 2]),
                              ALU.add).then_inc(sem["mod_sum"], 1)
            dve.wait_ge(sem["mod_sum"], 1)
            for i in range(2):
                dve.scalar_tensor_tensor(mod[:, KC:2 * KC, i], mod[:, KC:2 * KC, i], 1.0, g_col[:, 0, :],
                                         ALU.add, ALU.mult)
                last = dve.tensor_tensor(mod[:, 2 * KC:3 * KC, i], mod[:, 2 * KC:3 * KC, i], g_col[:, 1, :], ALU.mult)
            last.then_inc(sem["mod_out"], 1)
            dve.wait_ge(sem["mod_out"], 1)
            dve.wait_ge(sem["causal"], 1)
            dve.wait_ge(sem["scan_m"], 2)
            dve.wait_ge(sem["kcache_t"], 1)
            dve.tensor_copy(kA_s[:, CHUNK:P], bank4[:, 0:CHUNK]).then_inc(sem["cache_kA"], 1)

            def split_lo(units):
                for kind, i in units:
                    n = unit_number(kind, i)
                    slot = UNITS[n][2]
                    col, _, w = IN_UNITS[i] if kind == "in" else (i * UNIT, 0, UNIT)
                    hi, lo = (w_hi, w_lo) if kind == "in" else (wo_hi, wo_lo)
                    dve.wait_ge(w_half, n - ADA_UNITS + 1)
                    dve.scalar_tensor_tensor(lo[:, :, col:col + w],
                                             slots[slot][:, 0:KC * w].rearrange("p (c n) -> p c n", c=KC), WSCALE,
                                             hi[:, :, col:col + w], ALU.mult, ALU.subtract).then_inc(w_split, 1)

            def h_f32(t, cond):
                dve.wait_ge(sem["xt_mm"], t + 1)
                for cc in range(KC):
                    last = dve.tensor_scalar(h_ch[:, cc, :], pairP_c[:, cc, :], mod[:, KC + cc, cond:cond + 1],
                                             mod[:, cc, cond:cond + 1], ALU.mult, ALU.add)
                last.then_inc(sem["h_f32"], 1)

            def h_lo(t, par):
                dve.wait_ge(sem["h_hi"], t + 1)
                dve.tensor_tensor(hT[:, par, 1, :, :], h_ch, hT[:, par, 0, :, :], ALU.subtract).then_inc(sem["h_lo"], 1)

            h_f32(0, 0)
            h_lo(0, 0)
            split_lo([("in", i) for i in range(4)])

            def program(c):
                t, par = c.t, c.par
                if c.prev:
                    dve.wait_ge(sem["o_rs"], t)
                    dve.wait_ge(sem["gg_g"], t)
                    for hd in range(GH):
                        o = slice(hd * DV, (hd + 1) * DV)
                        last = dve.scalar_tensor_tensor(gates[:, o], bank7[:, o], o_r[:, hd:hd + 1], gates[:, o],
                                                        ALU.mult, ALU.mult)
                    last.then_inc(sem["mix_gla"], 1)
                    dve.wait_ge(sem["u_mm"], t)
                    st = S_s if c.after else S
                    for q in range(2):
                        r = slice(DK * q, DK * (q + 1))
                        for b in range(2):
                            last = dve.scalar_tensor_tensor(st[r, b, q, :], st[r, b, q, :], fac[r, b, 5:6],
                                                            u_ps[r, b, :], ALU.mult, ALU.add)
                    last.then_inc(sem["s_upd"], 1)
                if c.second or c.after:
                    cond = 0 if c.second else 1
                    if c.after:
                        dve.wait_ge(y_stored[0], 16 * (NT // 2))
                    dve.tensor_tensor(gate_diag, ident[:, :].unsqueeze(1).to_broadcast([P, KC, P]),
                                      mod[:, 2 * KC:3 * KC, cond].unsqueeze(2).to_broadcast([P, KC, P]),
                                      ALU.mult).then_inc(sem["gdiag_d"], 1)
                if c.first:
                    split_lo([("in", 4), ("in", 5), ("in", 6), ("in", 7)])
                if c.prev:
                    dve.wait_ge(sem["pv_mm"], t)
                    dve.tensor_tensor(gates[:, 512:1024], bank6[:, :], gates[:, 512:1024], ALU.mult)\
                       .then_inc(sem["mix_swa"], 1)
                if c.first:
                    split_lo([("in", 8), ("in", 9)])
                if c.prev:
                    dve.wait_ge(sem["mixt_hi"], t)
                    dve.tensor_tensor(mixT[:, 1, :, :], pairP_c, mixT[:, 0, :, :], ALU.subtract)\
                       .then_inc(sem["mixt_lo"], 1)
                if c.cur:
                    if c.first:
                        split_lo([("in", 10), ("in", 11)])
                    dve.wait_ge(sem["z_l"], t + 1)
                    if c.prev:
                        dve.wait_ge(sem["a_mm"], t)
                    dve.scalar_tensor_tensor(la[:, :, :], z_ch, 0.0, lsp[:, :, :], ALU.min, ALU.subtract)\
                       .then_inc(sem["la_d"], 1)
                    dve.wait_ge(sem["la_d"], t + 1)
                    dve.tensor_tensor_scan(bsum[:, :, :].rearrange("p b k -> p (b k)"), scan_mask[:, :],
                                           la[:, :, :].rearrange("p b k -> p (b k)"), 0.0, ALU.mult, ALU.add)\
                       .then_inc(sem["scan"], 1)
                    dve.wait_ge(sem["scan"], t + 1)
                    refs = bsum[:, :, :].rearrange("p b (h k) -> p b h k", h=2)[:, :, :, MID0:MID0 + 1]
                    dve.tensor_tensor(q_d[:, :, :].rearrange("p b (h k) -> p b h k", h=2),
                                      bsum[:, :, :].rearrange("p b (h k) -> p b h k", h=2),
                                      refs.to_broadcast([P, 2, 2, CHUNK]), ALU.subtract).then_inc(sem["bc_d"], 1)
                    end = DEC_SEQ - 1 if c.sample else P - 1
                    ref2 = refs.squeeze(3)
                    dve.tensor_copy(fac_in[:, :, 0:2], ref2)
                    dve.tensor_tensor(fac_in[:, :, 2:4], bsum[:, :, end:end + 1].to_broadcast([P, 2, 2]), ref2,
                                      ALU.subtract)
                    dve.tensor_tensor(fac_in[:, :, 4], bsum[:, :, MID1], bsum[:, :, MID0], ALU.subtract)
                    dve.tensor_copy(fac_in[:, :, 5], bsum[:, :, end]).then_inc(sem["fac_d"], 1)
                    dve.wait_ge(sem["qks_mm"], t + 1)
                    dve.tensor_copy(qT[:, :, :, :].rearrange("p c b k -> p b c k"),
                                    pairQ[:, 0:512].rearrange("p (b c k) -> p b c k", b=4, c=2))
                    if c.first:
                        dve.memset(kA[:, 0, CHUNK:P], 0.0)
                    ka = kA_s[:, :] if c.sample else kA[:, par, :]
                    dve.tensor_copy(ka[:, 0:CHUNK], pairQ[:, 512:512 + CHUNK])
                    if c.next:
                        dve.tensor_copy(kA[:, 1 - par, CHUNK:P], pairQ[:, 512 + CHUNK:512 + P])
                    dve.tensor_copy(kB[:, :], pairQ[:, 512:512 + P]).then_inc(sem["qks_ev"], 1)
                    dve.wait_ge(sem["e_pos"], t + 1)
                    dve.scalar_tensor_tensor(q_d[:, :, :], qk_ch[:, 0:2, :], DESCALE * DK ** -0.5, q_d[:, :, :],
                                             ALU.mult, ALU.mult)
                    dve.scalar_tensor_tensor(k_d[:, :, :], qk_ch[:, 2:4, :], DESCALE, k_d[:, :, :],
                                             ALU.mult, ALU.mult).then_inc(sem["qk_d"], 1)
                if c.prev:
                    dve.wait_ge(sem["y_rs"], t)
                    dve.scalar_tensor_tensor(y_buf[1 - par], pairP[:, :], y_r[:, :], gate_row, ALU.mult, ALU.mult)\
                       .then_inc(sem["y_mul"], 1)
                if not c.cur:
                    return
                if c.first:
                    split_lo([("out", i) for i in range(OUT_UNITS)])
                dve.wait_ge(sem["sc_mm"], t + 1)
                if c.first:
                    dve.memset(probs[:, 0:2, CHUNK:P], 0.0)
                    dve.memset(probs[:, 4:6, CHUNK:P], 0.0).then_inc(sem["zeroed"], 1)
                    for g in range(GROUPS):
                        w = CHUNK if g % 4 < 2 else P
                        last = dve.tensor_reduce(smax[:, g:g + 1], scores[:, g, 0:w], AX_X, ALU.max)
                else:
                    dve.tensor_reduce(smax[:, 0:4], scores[:, 0:4, :], AX_X, ALU.max)
                    last = dve.tensor_reduce(smax[:, 4:8], scores[:, 4:8, :], AX_X, ALU.max)
                last.then_inc(sem["smax"], 1)
                dve.wait_ge(sem["smax"], t + 1)
                dve.scalar_tensor_tensor(m_pos[:, :], smax[:, :], HD ** -0.5, sinks[:, :], ALU.mult, ALU.max)\
                   .then_inc(sem["m_pos"], 1)
                dve.wait_ge(sem["m_pos"], t + 1)
                dve.tensor_scalar(m_neg[:, :], m_pos[:, :], -1.0, None, ALU.mult).then_inc(sem["m_neg"], 1)
                dve.tensor_tensor(sink_d[:, :], sinks[:, :], m_pos[:, :], ALU.subtract).then_inc(sem["sink_d"], 1)
                dve.wait_ge(sem["gg_e"], t + 1)
                dve.tensor_scalar(etmp[:, :], etmp[:, :], 1.0, None, ALU.add).then_inc(sem["gg_1"], 1)
                dve.wait_ge(sem["gg_1"], t + 1)
                dve.reciprocal(etmp[:, :], etmp[:, :]).then_inc(sem["gg_r"], 1)
                dve.wait_ge(sem["gg_r"], t + 1)
                dve.scalar_tensor_tensor(gates[:, 0:512], bank7[:, :], DESCALE, etmp[:, :], ALU.mult, ALU.mult)\
                   .then_inc(sem["gg_x"], 1)
                dve.wait_ge(sem["a_mm"], t + 1)
                if c.first:
                    dve.memset(aT[64:128, :, :, 0:64], 0.0)
                if c.prev:
                    dve.wait_ge(sem["u_mm"], t)
                for q in range(2):
                    dve.tensor_tensor(aT[0:64, :, q, :], a_ps[q][0:64, :, :],
                                      causal[0:64, :].unsqueeze(1).to_broadcast([64, 2, P]), ALU.mult)
                    dve.tensor_tensor(aT[64:128, :, q, 64:128], a_ps[q][64:128, :, 64:128],
                                      causal[64:128, 64:128].unsqueeze(1).to_broadcast([64, 2, 64]), ALU.mult)
                dve.tensor_copy(k_tok[:, :, :], kt_ps).then_inc(sem["at_d"], 1)
                if c.next:
                    h_f32(t + 1, int(c.last))
                dve.wait_ge(sem["p_exp"], t + 1)
                dve.tensor_tensor(den[:, :], row_sum[:, :], sink_e[:, :], ALU.add).then_inc(sem["den"], 1)
                dve.wait_ge(sem["den"], t + 1)
                dve.reciprocal(rden[:, :], den[:, :]).then_inc(sem["rden"], 1)
                if c.next:
                    h_lo(t + 1, 1 - par)
                dve.wait_ge(sem["sg_e"], t + 1)
                dve.tensor_scalar(etmp[:, :], etmp[:, :], 1.0, None, ALU.add).then_inc(sem["sg_1"], 1)
                dve.wait_ge(sem["sg_1"], t + 1)
                dve.reciprocal(etmp[:, :], etmp[:, :]).then_inc(sem["sg_r"], 1)
                dve.wait_ge(sem["sg_r"], t + 1)
                dve.scalar_tensor_tensor(gates[:, 512:1024], bank6[:, :], DESCALE, etmp[:, :], ALU.mult, ALU.mult)\
                   .then_inc(sem["sg_g"], 1)

            all_tiles(dve, program, 2)

        @block.gpsimd
        def _(pool):
            pool.memset(ident[:, :], 0.0).then_inc(sem["ident_z"], 1)
            pool.memset(causal[:, :], 1.0).then_inc(sem["mask_z"], 1)
            pool.memset(scan_mask[:, :], 1.0).then_inc(sem["scan_z"], 1)
            pool.wait_ge(sem["ident_z"], 1)
            pool.affine_select(out=ident[:, :], in_=ident[:, :], compare_op=ALU.not_equal, fill=1.0, base=0,
                               pattern=[[-1, P]], channel_multiplier=1).then_inc(sem["ident"], 1)
            pool.wait_ge(sem["mask_z"], 1)
            pool.affine_select(out=causal[:, :], in_=causal[:, :], compare_op=ALU.is_ge, fill=0.0, base=0,
                               pattern=[[1, P]], channel_multiplier=-1).then_inc(sem["causal"], 1)
            pool.wait_ge(sem["scan_z"], 1)
            pool.memset(scan_mask[:, 0:2 * P:P], 0.0).then_inc(sem["scan_m"], 1)
            pool.memset(S[:, :, :, :], 0.0).then_inc(sem["scan_m"], 1)

            def norm_x(t, par):
                pool.wait_ge(sem["x_rs"], t + 1)
                if not isinstance(t, int) or t >= 1:
                    pool.wait_ge(sem["h_lo"], t)
                pool.tensor_tensor(xs[:, :], x_in[:, par, :], x_r[:, par:par + 1].to_broadcast([P, D]), ALU.mult)\
                    .then_inc(sem["xs"], 1)

            norm_x(0, 0)

            def program(c):
                t, par = c.t, c.par
                if c.cur:
                    pool.wait_ge(sem["ksg_ev"], t + 1)
                    pool.wait_ge(sem["sq_ev"], t + 1)
                    pool.wait_ge(x_loaded[par], 32 * (c.half + 1))
                    rot = qk_tok[:, :, :].rearrange("p b (g k) -> p (b g) k", g=2)
                    x1, x2 = rot[:, :, 0:ROPE_HALF], rot[:, :, ROPE_HALF:2 * ROPE_HALF]
                    cos = trig_in[:, par, 0:ROPE_HALF].unsqueeze(1).to_broadcast([P, 10, ROPE_HALF])
                    sin = trig_in[:, par, ROPE_HALF:].unsqueeze(1).to_broadcast([P, 10, ROPE_HALF])
                    pool.tensor_tensor(rope_cos[:, :, 0, :], x1, cos, ALU.mult)
                    pool.tensor_tensor(rope_cos[:, :, 1, :], x2, cos, ALU.mult)
                    pool.tensor_tensor(rope_sin[:, :, 0, :], x2, sin, ALU.mult)
                    pool.tensor_tensor(rope_sin[:, :, 1, :], x1, sin, ALU.mult).then_inc(sem["rope_m"], 1)
                    pool.wait_ge(sem["rope_m"], t + 1)
                    pool.tensor_tensor(x1, rope_cos[:, :, 0, :], rope_sin[:, :, 0, :], ALU.subtract)
                    pool.tensor_tensor(x2, rope_cos[:, :, 1, :], rope_sin[:, :, 1, :], ALU.add).then_inc(sem["rope"], 1)
                if c.next:
                    norm_x(t + 1, 1 - par)
                if c.cur:
                    pool.wait_ge(sem["qk_d"], t + 1)
                    pool.wait_ge(sem["fac_e"], t + 1)
                    def halves(a):
                        return a[:, :, :].rearrange("p b (h k) -> p b h k", h=2)
                    pool.tensor_tensor(k_off[:, :, :], k_d[:, :, 0:CHUNK],
                                       fac[:, :, 4:5].to_broadcast([P, 2, CHUNK]), ALU.mult)
                    pool.tensor_tensor(halves(q_int), halves(q_d),
                                       fac[:, :, 0:2].unsqueeze(3).to_broadcast([P, 2, 2, CHUNK]), ALU.mult)
                    pool.tensor_tensor(halves(k_out), halves(k_d),
                                       fac[:, :, 2:4].unsqueeze(3).to_broadcast([P, 2, 2, CHUNK]), ALU.mult)\
                        .then_inc(sem["gla_sc"], 1)
                if c.prev:
                    pool.wait_ge(sem["y_mul"], t)
                    pool.wait_ge(sem["res_copied"], 16 * t)
                    pool.tensor_tensor(y_buf[1 - par], y_buf[1 - par], x_res[:, :], ALU.add).then_inc(sem["y_final"], 1)
                if not c.cur:
                    return
                pool.wait_ge(sem["rden"], t + 1)
                pool.tensor_tensor(probs, probs, rden[:, :].unsqueeze(2).to_broadcast([P, GROUPS, P]), ALU.mult)\
                    .then_inc(sem["probs"], 1)
                pool.wait_ge(sem["gg_x"], t + 1)
                gg = gates[:, 0:512].rearrange("p (h v) -> p h v", h=GH)
                pool.tensor_tensor(gg, gg, gnorm[:, :].unsqueeze(1).to_broadcast([P, GH, DV]), ALU.mult)\
                    .then_inc(sem["gg_g"], 1)

            all_tiles(pool, program, 2)


_INS = ["x_prompt", "x_sample", "c_prompt", "c_sample", "state_gla", "cache_swa_k", "cache_swa_v", "w_ada", "b_ada",
        "g_pre", "g_post", "w_in", "w_alpha", "b_alpha", "gla_norm_g", "swa_sinks", "w_out"]
_OUTS = [(1, SEQ, D), (1, DEC_SEQ, D), (1, 1, GH, DK, DV), (1, 1, P, KVH, HD), (1, 1, P, KVH, HD),
         (1, 1, GH, DK, DV), (1, 1, P, KVH, HD), (1, 1, P, KVH, HD)]


def rotary_table():
    import numpy as np
    inv = np.float32(500000.0) ** (-np.arange(ROPE_HALF, dtype=np.float32) * np.float32(2.0) / np.float32(16.0))
    pos = np.concatenate([np.arange(SEQ), PAST + np.arange(P)]).astype(np.float32)
    ang = (pos[:, None] * inv[None, :]).astype(np.float32)
    return np.concatenate([np.cos(ang), np.sin(ang)], axis=1).astype(np.float32)


def kernel(**inputs):
    import numpy as np
    import concourse.bacc as bacc
    from concourse.bass_utils import run_bass_kernel_spmd as run

    nc = bacc.Bacc("TRN2", target_bir_lowering=False, num_devices=1)
    arrays, args = {}, []
    for name in _INS:
        a = np.ascontiguousarray(inputs[name])
        arrays[f"in_{name}"] = a
        args.append(nc.dram_tensor(f"in_{name}", a.shape, F32, kind="ExternalInput").ap())
    arrays["rotary"] = rotary_table()
    args.append(nc.dram_tensor("rotary", arrays["rotary"].shape, F32, kind="ExternalInput").ap())
    for i, shape in enumerate(_OUTS):
        args.append(nc.dram_tensor(f"out_{i}", shape, F32, kind="ExternalOutput").ap())
    hybrid_layer(nc, *args)
    r = run(nc, [arrays], core_ids=[0])
    return tuple(r.results[0][f"out_{i}"] for i in range(len(_OUTS)))
```

```python
from contextlib import ExitStack

import concourse.bass as bass
from concourse import mybir

F32 = mybir.dt.float32
F16 = mybir.dt.float16
ALU = mybir.AluOpType
ACT = mybir.ActivationFunctionType
AX_X = mybir.AxisListType.X

P = 128
D = 1024
KC = D // P
SEQ, DEC_SEQ, PAST = 4096, 64, 1024
CHUNK = 64
NT = SEQ // P
LOOP_END = NT - 2
EPS = 1e-6
GH, DK, DV = 4, 64, 128
LOWRANK = 16
TAU = 16.0
HEADS, KVH, HD = 8, 2, 64
ROPE_HALF = HD // 8
GROUPS = 8
WSCALE = 64.0
DESCALE = 1.0 / WSCALE
MID0, MID1 = 32, 96

C_GQ, C_GK, C_GV, C_GG, C_GA, C_SQ, C_SK, C_SV, C_SG, C_END = (
    0, 256, 512, 1024, 1536, 1552, 2064, 2192, 2320, 2832)
W_QK, W_KSG, W_SQ, W_V, W_GG, W_SG = 0, 512, 784, 1296, 1808, 2320
KSG = 272
UNIT = 256
IN_UNITS = [(W_QK, C_GQ, 256), (W_QK + 256, C_GK, 256),
            (W_KSG, C_SK, 256), (W_KSG + 256, C_GA, 16),
            (W_SQ, C_SQ, 256), (W_SQ + 256, C_SQ + 256, 256),
            (W_V, C_GV, 256), (W_V + 256, C_GV + 256, 256),
            (W_GG, C_GG, 256), (W_GG + 256, C_GG + 256, 256),
            (W_SG, C_SG, 256), (W_SG + 256, C_SG + 256, 256)]
ADA_UNITS = 3 * D // UNIT
OUT_UNITS = D // UNIT
UNITS = [("ada", i, slot) for i, slot in enumerate((7, 8, 9, 10, 11, 12, 13, 14, 15, 16, 0, 1))]
UNITS += [("in", i, slot) for i, slot in enumerate((3, 4, 5, 6, 2, 0, 1, 3, 4, 5, 6, 0))]
UNITS += [("out", i, slot) for i, slot in enumerate((1, 0, 1, 0))]
SLOTS = 17


def slot_use(n):
    return sum(1 for u in UNITS[:n] if u[2] == UNITS[n][2])


def unit_number(kind, i):
    return [u[:2] for u in UNITS].index((kind, i))


def split_number(kind, i):
    return i if kind == "in" else len(IN_UNITS) + i


class Tile:

    def __init__(self, t, half, par):
        peeled = isinstance(t, int)
        self.t, self.half, self.par = t, half, par
        self.prev = not (peeled and t == 0)
        self.cur = not (peeled and t == NT + 1)
        self.next = not (peeled and t >= NT)
        self.first = peeled and t == 0
        self.second = peeled and t == 1
        self.last = peeled and t == NT - 1
        self.sample = peeled and t == NT
        self.after = peeled and t == NT + 1


def hybrid_layer(nc, x_prompt, x_sample, c_prompt, c_sample, state_gla, cache_k, cache_v, w_ada, b_ada, g_pre,
                 g_post, w_in, w_alpha, b_alpha, gla_norm_g, swa_sinks, w_out, trig,
                 y_prompt, y_sample, st_prompt, k_prompt, v_prompt, st_sample, k_sample, v_sample):
    ctx = ExitStack()
    with ctx:
        ctx.enter_context(nc.allow_non_contiguous_dma(reason="small column vectors, once"))

        def sb(name, shape, dt=F32):
            return ctx.enter_context(nc.sbuf_tensor(name, shape, dt))

        def psum(name, shape):
            return ctx.enter_context(nc.psum_tensor(name, shape, F32))

        w_hi = sb("w_hi", [P, KC, C_END], F16)
        w_lo = sb("w_lo", [P, KC, C_END], F16)
        wo_hi = sb("wo_hi", [P, KC, D], F16)
        wo_lo = sb("wo_lo", [P, KC, D], F16)
        stage = sb("stage", [P, 4 * D])
        late = sb("late", [P, 2 * D])
        slots = [stage[:, 0:2 * D], stage[:, 2 * D:4 * D], late[:, :]]
        for home, n in ((wo_lo, 2), (wo_hi, 2), (w_hi, 5), (w_lo, 5)):
            flat = home[:, :, :].rearrange("p c n -> p (c n)").bitcast(F32)
            slots += [flat[:, 2 * D * i:2 * D * (i + 1)] for i in range(n)]
        gate_row = stage[:, 0:D]
        y_buf = [stage[:, 2 * D:3 * D], stage[:, 3 * D:4 * D]]
        gate_diag = y_buf[0].rearrange("p (c k) -> p c k", c=KC)
        probs = late[:, 0:D].rearrange("p (g k) -> p g k", g=GROUPS)
        probsT = late[:, D:2 * D].rearrange("p (g k) -> p g k", g=GROUPS)
        mixT = late[:, D:2 * D].bitcast(F16).rearrange("p (s c k) -> p s c k", s=2, c=KC)
        x_in = sb("x_in", [P, 2, D])
        x_res = sb("x_res", [P, D])
        trig_in = sb("trig_in", [P, 2, 2 * ROPE_HALF])
        xs = sb("xs", [P, D])
        h_ch = xs[:, :].rearrange("p (c k) -> p c k", c=KC)
        hT = sb("hT", [P, 2, 2, KC, P], F16)
        v_tok = sb("v_tok", [P, GH * DV])
        qk_tok = sb("qk_tok", [P, 5, P])
        ga_tok = sb("ga_tok", [P, LOWRANK])
        rope_cos = sb("rope_cos", [P, 10, 2, ROPE_HALF])
        rope_sin = sb("rope_sin", [P, 10, 2, ROPE_HALF])
        qT = sb("qT", [P, 2, 4, CHUNK])
        kA = sb("kA", [P, 2, P])
        kA_s = sb("kA_s", [P, P])
        kB = sb("kB", [P, P])
        vA = sb("vA", [P, 2, P])
        vA_s = sb("vA_s", [P, P])
        vB = sb("vB", [P, 2, P])
        gates = sb("gates", [P, D])
        etmp = sb("etmp", [P, 512])
        lsp = sb("lsp", [P, 2, P])
        la = sb("la", [P, 2, P])
        bsum = sb("bsum", [P, 2, P])
        q_d = sb("q_d", [P, 2, P])
        k_d = sb("k_d", [P, 2, P])
        q_int, k_out = lsp, la
        k_off = sb("k_off", [P, 2, CHUNK])
        k_tok = sb("k_tok", [P, 2, P])
        aT = sb("aT", [P, 2, 2, P])
        S = sb("S", [P, 2, 2, DV])
        S_s = sb("S_s", [P, 2, 2, DV])
        fac_in = sb("fac_in", [P, 2, 6])
        fac = sb("fac", [P, 2, 6])
        ident = sb("ident", [P, P])
        causal = sb("causal", [P, P])
        scan_mask = sb("scan_mask", [P, 2 * P])
        gnorm = sb("gnorm", [P, DV])
        w_al = sb("w_al", [LOWRANK + 1, GH * DK])
        gaT = sb("gaT", [32, P])
        cache_k_tok = sb("cache_k_tok", [CHUNK, P])
        sinks = sb("sinks", [P, GROUPS])
        c_tmp = sb("c_tmp", [P, 2, KC])
        c_silu = sb("c_silu", [P, KC, 2])
        bg_col = sb("bg_col", [P, 5 * KC])
        mod = sb("mod", [P, 3 * KC, 2])
        x_ss = sb("x_ss", [P, 2])
        x_ln = sb("x_ln", [P, 1])
        x_r = sb("x_r", [P, 2])
        o_ss = sb("o_ss", [P, 4])
        o_ln = sb("o_ln", [P, 4])
        o_r = sb("o_r", [P, 4])
        y_ss = sb("y_ss", [P, 1])
        y_ln = sb("y_ln", [P, 1])
        y_r = sb("y_r", [P, 1])
        smax = sb("smax", [P, GROUPS])
        m_pos = sb("m_pos", [P, GROUPS])
        m_neg = sb("m_neg", [P, GROUPS])
        sink_d = sb("sink_d", [P, GROUPS])
        sink_e = sb("sink_e", [P, GROUPS])
        row_sum = sb("row_sum", [P, GROUPS])
        den = sb("den", [P, GROUPS])
        rden = sb("rden", [P, GROUPS])
        junk = sb("junk", [P, GH * DV], F16)
        eps = sb("eps", [P, 1])
        ln_scale = sb("ln_scale", [P, 1])

        pairP = psum("pairP", [P, 2 * 512])
        pairQ = psum("pairQ", [P, 2 * 512])
        bank4 = psum("bank4", [P, 512])
        bank5 = psum("bank5", [P, 512])
        bank6 = psum("bank6", [P, 512])
        bank7 = psum("bank7", [P, 512])
        pairP_c = pairP[:, :].rearrange("p (c k) -> p c k", c=KC)
        scores = pairQ[:, :].rearrange("p (g k) -> p g k", g=GROUPS)
        qk_ch = bank4[:, :].rearrange("p (b k) -> p b k", b=4)
        z_ch = bank5[:, 0:256].rearrange("p (b k) -> p b k", b=2)
        a_ps = [bank5[:, 0:256].rearrange("p (b k) -> p b k", b=2), bank4[:, 0:256].rearrange("p (b k) -> p b k", b=2)]
        kt_ps = bank4[:, 256:512].rearrange("p (b k) -> p b k", b=2)
        u_ps = pairQ[:, 640:896].rearrange("p (b k) -> p b k", b=2)
        c_rows, bg_rows = etmp[0:2 * KC, 0:P], etmp[0:5 * KC, P:2 * P]
        c_ps = bank5[:, 64:64 + 2 * KC].rearrange("p (n c) -> p n c", n=2)
        bg_ps = bank5[:, 128:128 + 5 * KC]
        mod_ps = bank5[:, 0:6 * KC].rearrange("p (b c) -> p b c", c=2)
        rows_ps = [pairQ[0:2, 0:512], pairQ[0:2, 512:1024], bank6[0:2, :], bank7[0:2, :], bank4[0:2, :],
                   pairQ[0:2, 0:512]]
        mod_rows = [gates[0:2, 0:512], gates[0:2, 512:1024], v_tok[0:2, :],
                    qk_tok[0:2, 0:4, :].rearrange("p b k -> p (b k)"),
                    aT[0:2, :, :, :].rearrange("p b q k -> p (b q k)"), etmp[0:2, :]]

        sem = {}
        for name in ("c_load bg_load const_load c_t bg_t bg_ev rows_ev rows_t c_exp c_one c_rec c_silu eps_set ident_z ident mask_z causal scan_z scan_m "
                     "ss_zero gaT_one sinks mod_mm mod_sum mod_out zeroed kcache_t cache_kA gdiag_d gate_bc gate_row "
                     "x_sq x_lnd x_rs xs h_f32 h_hi h_lo res_copied y_final out_stored qk_mm ksg_mm pv_mm sq_mm gat_mm "
                     "mixt_mm v_mm z_mm qks_mm out_mm sc_mm gg_mm xt_mm a_mm sg_mm o_mm u_mm pt_mm ksg_ev sq_ev gat_ev "
                     "pt_ev mixt_hi mixt_lo v_ev qks_ev rope_m rope_s rope va_prev z_abs z_e z_l la_d scan bc_d fac_d "
                     "fac_e e_pos e_neg qk_d k_off gla_sc at_d kt_ev s_upd o_sq o_lnd o_rs mix_gla mix_swa smax m_pos "
                     "m_neg sink_d sink_e p_exp den rden probs gg_e gg_1 gg_r gg_x gg_g sg_e sg_1 sg_r sg_g y_sq y_lnd "
                     "y_rs y_mul").split():
            sem[name] = ctx.enter_context(nc.semaphore(name))
        staged = [ctx.enter_context(nc.semaphore(f"staged{i}")) for i in range(SLOTS)]
        x_loaded = [ctx.enter_context(nc.semaphore(f"x_loaded{i}")) for i in range(2)]
        y_stored = [ctx.enter_context(nc.semaphore(f"y_stored{i}")) for i in range(2)]
        w_split = ctx.enter_context(nc.semaphore("w_split"))
        w_half = ctx.enter_context(nc.semaphore("w_half"))

        def all_tiles(eng, program, peel):
            for t in range(peel):
                program(Tile(t, t // 2, t % 2))
            with eng.Fori(peel // 2, LOOP_END // 2) as k:
                program(Tile(k * 2, k, 0))
                program(Tile(k * 2 + 1, k, 1))
            for t in range(LOOP_END, NT + 2):
                program(Tile(t, t // 2, t % 2))

        in_units_before = {W_KSG: 4, W_SQ: 6, W_V: 8, W_GG: 10, W_SG: 12}
        block = ctx.enter_context(nc.Block())

        @block.sync
        def _(sp):
            def load_x(t, par):
                if isinstance(t, int) and t == NT:
                    sp.dma_start(x_in[0:DEC_SEQ, par, :], x_sample[0]).then_inc(x_loaded[par], 16)
                else:
                    sp.dma_start(x_in[:, par, :], x_prompt[0, bass.ds(t * P, P), :]).then_inc(x_loaded[par], 16)
                sp.dma_start(trig_in[:, par, :], trig[bass.ds(t * P, P), :]).then_inc(x_loaded[par], 16)

            def load_const(dst, src, loaded):
                sp.dma_start(dst, src).then_inc(sem[loaded], 16)

            def load_constants():
                load_const(gnorm[:, :], gla_norm_g[0].partition_broadcast(P), "const_load")
                load_const(w_al[0:LOWRANK, :], w_alpha[0], "const_load")
                load_const(w_al[LOWRANK:LOWRANK + 1, :], b_alpha, "const_load")
                load_const(cache_k_tok[:, :], cache_k[0, 0, CHUNK:2 * CHUNK].rearrange("t h d -> t (h d)"),
                           "const_load")
                load_const(vA_s[CHUNK:P, :], cache_v[0, 0, CHUNK:2 * CHUNK].rearrange("t h d -> t (h d)"),
                           "const_load")
                sp.wait_ge(sem["ss_zero"], 1)
                for q in range(2):
                    load_const(S_s[DK * q:DK * q + DK, :, q, :],
                               state_gla[0, 0].rearrange("(b q) k v -> q k b v", q=2)[q], "const_load")
                sink_v = swa_sinks[0].rearrange("(g pp e) -> e g pp", g=KVH, pp=2)
                sink_d4 = sinks[:, :].rearrange("p (g c pp) -> p g c pp", g=KVH, c=2)
                for e in range(2):
                    for g in range(KVH):
                        for ch in range(2):
                            load_const(sink_d4[CHUNK * e:CHUNK * (e + 1), g, ch, :],
                                       sink_v[e, g].partition_broadcast(CHUNK), "const_load")

            for i, cvec in enumerate((c_prompt, c_sample)):
                load_const(c_rows[KC * i:KC * (i + 1), :], cvec.rearrange("o (c p) -> (o c) p", p=P), "c_load")
            for n, (kind, i, slot) in enumerate(UNITS):
                before = [u for u in UNITS[:n] if u[2] == slot]
                if before and before[-1][0] == "ada":
                    sp.wait_ge(sem["mod_mm"], before[-1][1] + 1)
                elif before:
                    sp.wait_ge(w_split, split_number(*before[-1][:2]) + 1)
                if kind == "ada":
                    src, w = w_ada[0, :, i * UNIT:(i + 1) * UNIT], UNIT
                elif kind == "in":
                    src, w = w_in[0, :, IN_UNITS[i][1]:IN_UNITS[i][1] + IN_UNITS[i][2]], IN_UNITS[i][2]
                else:
                    src, w = w_out[0, :, i * UNIT:(i + 1) * UNIT], UNIT
                dst = slots[slot][:, 0:KC * w].rearrange("p (c n) -> p c n", c=KC)
                sp.dma_start(dst, src.rearrange("(c p) n -> p c n", p=P)).then_inc(staged[slot], 16)
                if (kind, i) == ("ada", 0):
                    load_x(0, 0)
                    load_const(bg_rows[0:3 * KC, :], b_ada.rearrange("o (c p) -> (o c) p", p=P), "bg_load")
                    for j, g in enumerate((g_pre, g_post)):
                        load_const(bg_rows[(3 + j) * KC:(4 + j) * KC, :], g.rearrange("o (c p) -> (o c) p", p=P),
                                   "bg_load")
                if (kind, i) == ("ada", 9):
                    load_constants()
                if (kind, i) == ("in", 7):
                    load_x(1, 1)
            sp.dma_start(k_sample[0, 0, 0:CHUNK], cache_k[0, 0, CHUNK:2 * CHUNK]).then_inc(sem["out_stored"], 16)
            sp.dma_start(v_sample[0, 0, 0:CHUNK], cache_v[0, 0, CHUNK:2 * CHUNK]).then_inc(sem["out_stored"], 16)

            def program(c):
                if c.prev:
                    sp.wait_ge(sem["y_final"], c.t)
                    src = y_buf[1 - c.par]
                    if c.after:
                        sp.dma_start(y_sample[0], src[0:DEC_SEQ, :]).then_inc(y_stored[1 - c.par], 16)
                    else:
                        sp.dma_start(y_prompt[0, bass.ds((c.t - 1) * P, P), :], src).then_inc(y_stored[1 - c.par], 16)
                if c.cur:
                    sp.wait_ge(x_loaded[c.par], 32 * (c.half + 1))
                    sp.dma_start(x_res[:, :], x_in[:, c.par, :]).then_inc(sem["res_copied"], 16)
                if not isinstance(c.t, int) or c.t + 2 <= NT:
                    sp.wait_ge(sem["res_copied"], 16 * (c.t + 1))
                    sp.wait_ge(sem["xs"], c.t + 1)
                    sp.wait_ge(sem["rope"], c.t + 1)
                    load_x(c.t + 2, c.par)
                if c.last or c.sample:
                    n = P if c.last else DEC_SEQ
                    ko, vo = (k_prompt[0, 0], v_prompt[0, 0]) if c.last else (
                        k_sample[0, 0, CHUNK:], v_sample[0, 0, CHUNK:])
                    sp.wait_ge(sem["rope"], c.t + 1)
                    sp.wait_ge(sem["ksg_ev"], c.t + 1)
                    sp.dma_start(ko.rearrange("t h d -> t (h d)"), qk_tok[0:n, 4, :]).then_inc(sem["out_stored"], 16)
                    sp.dma_start(vo.rearrange("t h d -> t (h d)"), vB[0:n, c.par, :]).then_inc(sem["out_stored"], 16)
                if c.sample or c.after:
                    st, buf = (st_prompt, S) if c.sample else (st_sample, S_s)
                    sp.wait_ge(sem["s_upd"], c.t)
                    for q in range(2):
                        sp.dma_start(st[0, 0].rearrange("(b q) k v -> q k b v", q=2)[q],
                                     buf[DK * q:DK * q + DK, :, q, :]).then_inc(sem["out_stored"], 16)

            all_tiles(sp, program, 2)
            sp.wait_ge(sem["out_stored"], 16 * 10)
            sp.wait_ge(y_stored[0], 16 * (NT // 2 + 1))
            sp.wait_ge(y_stored[1], 16 * (NT // 2))

        @block.tensor
        def _(pe):
            def split_product(out, a, b):
                for c in range(KC):
                    for n, (i, j) in enumerate(((0, 0), (0, 1), (1, 0))):
                        last = pe.matmul(out, a(c, i), b(c, j), start=(c == 0 and n == 0),
                                         stop=(c == KC - 1 and n == 2))
                return last

            def modulation(units):
                for i in units:
                    n = unit_number("ada", i)
                    slot = UNITS[n][2]
                    pe.wait_ge(staged[slot], 16 * (slot_use(n) + 1))
                    w = slots[slot].rearrange("p (c n) -> p c n", c=KC)
                    for c in range(KC):
                        last = pe.matmul(rows_ps[i // 2][:, (i % 2) * UNIT:(i % 2 + 1) * UNIT], c_silu[:, c, :],
                                         w[:, c, :], start=(c == 0), stop=(c == KC - 1))
                    last.then_inc(sem["mod_mm"], 1)

            def rows_to_channels(banks):
                for n in banks:
                    pe.wait_ge(sem["rows_ev"], n + 1)
                    for k in range(4):
                        last = pe.transpose(mod_ps[:, 4 * n + k, :], mod_rows[n][:, k * P:(k + 1) * P],
                                            ident[0:2, 0:2])
                last.then_inc(sem["rows_t"], 1)

            pe.wait_ge(sem["c_load"], 16 * 2)
            pe.wait_ge(sem["ident"], 1)
            pe.transpose(bank5[:, 64:64 + 2 * KC], c_rows, ident[0:2 * KC, 0:2 * KC]).then_inc(sem["c_t"], 1)
            pe.wait_ge(sem["c_silu"], 1)
            modulation(range(1))
            pe.wait_ge(sem["bg_load"], 16 * 3)
            pe.transpose(bg_ps, bg_rows, ident[0:5 * KC, 0:5 * KC]).then_inc(sem["bg_t"], 1)
            modulation(range(1, 4))
            pe.wait_ge(sem["scan_m"], 2)
            pe.wait_ge(sem["xs"], 1)
            for c in range(KC):
                last = pe.transpose(pairP_c[:, c, :], xs[:, c * P:(c + 1) * P], ident[:, :])
            last.then_inc(sem["xt_mm"], 1)
            modulation(range(4, 9))
            rows_to_channels(range(4))
            modulation(range(9, 10))
            pe.wait_ge(sem["rows_ev"], 1)
            modulation(range(10, ADA_UNITS))
            pe.wait_ge(sem["const_load"], 16 * 15)
            pe.wait_ge(sem["rows_ev"], 5)
            pe.transpose(bank4[:, 0:CHUNK], cache_k_tok[:, :], ident[0:CHUNK, 0:CHUNK]).then_inc(sem["kcache_t"], 1)
            rows_to_channels((4, 5))

            def gate_to_rows(count):
                pe.wait_ge(sem["gdiag_d"], count)
                for n in range(2):
                    last = pe.matmul(pairP[:, 512 * n:512 * (n + 1)], scan_mask[:, 1:2].to_broadcast([P, P]),
                                     gate_diag[:, 4 * n:4 * n + 4, :], start=True, stop=True)
                last.then_inc(sem["gate_bc"], 1)

            def program(c):
                t, par = c.t, c.par

                def h(cc, i):
                    return hT[:, par, i, cc, :]

                def project(bank, width, col, done):
                    if c.first:
                        pe.wait_ge(w_split, in_units_before[col])
                    split_product(bank[:, 0:width], h,
                                  lambda cc, i: (w_hi, w_lo)[i][:, cc, col:col + width]).then_inc(done, 1)

                if c.cur:
                    pe.wait_ge(sem["h_lo"], t + 1)
                    if c.first:
                        pe.wait_ge(w_split, 2)
                        pe.wait_ge(sem["cache_kA"], 1)
                    else:
                        pe.wait_ge(sem["at_d"], t)
                    for b in range(4):
                        last = split_product(qk_ch[:, b, :],
                                             lambda cc, i: (w_hi, w_lo)[i][:, cc, W_QK + b * P:W_QK + (b + 1) * P], h)
                    last.then_inc(sem["qk_mm"], 1)
                if c.prev:
                    pe.wait_ge(sem["at_d"], t)
                    pe.wait_ge(sem["gg_x"], t)
                    pe.wait_ge(sem["v_ev"], t)
                    if not c.second:
                        pe.wait_ge(sem["s_upd"], t - 1)
                    st = S_s if c.after else S
                    for b in range(2):
                        pe.matmul(bank7[:, 2 * b * DV:2 * (b + 1) * DV], q_int[:, b, :], st[:, b, :, :],
                                  start=True, stop=False)
                        for q in range(2):
                            o = slice((2 * b + q) * DV, (2 * b + q + 1) * DV)
                            last = pe.matmul(bank7[:, o], aT[:, b, q, :], v_tok[:, o], start=False, stop=(q == 1))
                    last.then_inc(sem["o_mm"], 1)
                    n = DEC_SEQ if c.after else P
                    pe.wait_ge(sem["p_exp"], t)
                    for hd in range(GH):
                        b, q = hd // 2, hd % 2
                        last = pe.matmul(u_ps[DK * q:DK * (q + 1), b, :], k_tok[0:n, b, DK * q:DK * (q + 1)],
                                         v_tok[0:n, hd * DV:(hd + 1) * DV], start=True, stop=True)
                    last.then_inc(sem["u_mm"], 1)
                if c.prev:
                    pe.wait_ge(sem["probs"], t)
                    if c.after:
                        pe.wait_ge(sem["gate_row"], 2)
                    else:
                        pe.wait_ge(sem["h_f32"], t + 1)
                    for g in range(GROUPS):
                        last = pe.transpose(pairP_c[:, g, :], probs[:, g, :], ident[:, :])
                    last.then_inc(sem["pt_mm"], 1)
                if c.cur:
                    if c.first:
                        pe.wait_ge(sem["mod_sum"], 2)
                    project(bank5, KSG, W_KSG, sem["ksg_mm"])
                if c.prev:
                    pe.wait_ge(sem["pt_ev"], t)
                    pe.wait_ge(sem["sg_g"], t)
                    pe.wait_ge(sem["va_prev"], t)
                    for ch in range(2):
                        vsrc = vB[:, 1 - par, :] if ch else (vA_s[:, :] if c.after else vA[:, 1 - par, :])
                        for head in range(HEADS):
                            g, pp, e = head // 4, head % 4 // 2, head % 2
                            last = pe.matmul(bank6[CHUNK * ch:CHUNK * (ch + 1), head * HD:(head + 1) * HD],
                                             probsT[:, 4 * g + 2 * ch + pp, CHUNK * e:CHUNK * (e + 1)],
                                             vsrc[:, HD * g:HD * (g + 1)], start=True, stop=True)
                    last.then_inc(sem["pv_mm"], 1)
                if c.cur:
                    if c.prev:
                        pe.wait_ge(sem["mix_gla"], t)
                    project(bank7, 512, W_SQ, sem["sq_mm"])
                    pe.wait_ge(sem["ksg_ev"], t + 1)
                    pe.transpose(bank5[0:LOWRANK, 0:P], ga_tok[:, :], ident[:, :]).then_inc(sem["gat_mm"], 1)
                if c.second:
                    pe.wait_ge(sem["pt_ev"], 1)
                    gate_to_rows(1)
                    pe.wait_ge(sem["gate_row"], 1)
                if c.prev:
                    pe.wait_ge(sem["mix_swa"], t)
                    pe.wait_ge(sem["mix_gla"], t)
                    for cc in range(KC):
                        last = pe.transpose(pairP_c[:, cc, :], gates[:, cc * P:(cc + 1) * P], ident[:, :])
                    last.then_inc(sem["mixt_mm"], 1)
                if c.cur:
                    project(bank6, 512, W_V, sem["v_mm"])
                    pe.wait_ge(sem["gat_ev"], t + 1)
                    for b in range(2):
                        last = pe.matmul(z_ch[:, b, :], w_al[:, b * P:(b + 1) * P], gaT[0:LOWRANK + 1, :],
                                         start=True, stop=True)
                    last.then_inc(sem["z_mm"], 1)
                    pe.wait_ge(sem["rope"], t + 1)
                    if c.prev:
                        pe.wait_ge(sem["s_upd"], t)
                    for b in range(5):
                        last = pe.transpose(pairQ[:, b * P:(b + 1) * P], qk_tok[:, b, :], ident[:, :])
                    last.then_inc(sem["qks_mm"], 1)
                if c.prev:
                    pe.wait_ge(sem["mixt_lo"], t)
                    if c.second:
                        pe.wait_ge(w_split, len(IN_UNITS) + OUT_UNITS)
                    for n in range(2):
                        last = split_product(pairP[:, 512 * n:512 * (n + 1)], lambda cc, i: mixT[:, i, cc, :],
                                             lambda cc, i: (wo_hi, wo_lo)[i][:, cc, 512 * n:512 * (n + 1)])
                    last.then_inc(sem["out_mm"], 1)
                if not c.cur:
                    return
                pe.wait_ge(sem["qks_ev"], t + 1)
                for ch in range(2):
                    for pp in range(2):
                        for g in range(KVH):
                            kk = kB[:, :] if ch else (kA_s[:, :] if c.sample else kA[:, par, :])
                            last = pe.matmul(scores[:, 4 * g + 2 * ch + pp, :],
                                             qT[HD * g:HD * (g + 1), ch, 2 * pp:2 * pp + 2, :],
                                             kk[HD * g:HD * (g + 1), :], start=True, stop=True)
                last.then_inc(sem["sc_mm"], 1)
                pe.wait_ge(sem["sq_ev"], t + 1)
                project(bank7, 512, W_GG, sem["gg_mm"])
                if c.sample:
                    pe.wait_ge(sem["y_mul"], t)
                    gate_to_rows(2)
                if c.next:
                    pe.wait_ge(sem["xs"], t + 2)
                    if c.prev:
                        pe.wait_ge(sem["y_mul"], t)
                    for cc in range(KC):
                        last = pe.transpose(pairP_c[:, cc, :], xs[:, cc * P:(cc + 1) * P], ident[:, :])
                    last.then_inc(sem["xt_mm"], 1)
                pe.wait_ge(sem["gla_sc"], t + 1)
                for b in range(2):
                    pe.transpose(kt_ps[:, b, :], k_out[:, b, :], ident[:, :])
                for b in range(2):
                    for q in range(2):
                        r = slice(DK * q, DK * (q + 1))
                        pe.matmul(a_ps[q][0:64, b, 0:64], k_d[r, b, 0:64], q_d[r, b, 0:64], start=True, stop=True)
                        pe.matmul(a_ps[q][0:64, b, 64:128], k_off[r, b, :], q_d[r, b, 64:128], start=True, stop=True)
                        last = pe.matmul(a_ps[q][64:128, b, 64:128], k_d[r, b, 64:128], q_d[r, b, 64:128],
                                         start=True, stop=True)
                last.then_inc(sem["a_mm"], 1)
                pe.wait_ge(sem["v_ev"], t + 1)
                project(bank6, 512, W_SG, sem["sg_mm"])

            all_tiles(pe, program, 2)

        @block.scalar
        def _(act):
            act.preload_act_table_set("natural_log_exp_and_others")

            act.wait_ge(sem["c_t"], 1)
            act.activation(c_tmp[:, :, :], c_ps, ACT.Exp, scale=-1.0).then_inc(sem["c_exp"], 1)

            def rsqrt_of(dst, tmp, ssum, n, ln_done, done, count, scale_out=None):
                act.activation(tmp, ssum, ACT.Ln, bias=eps[:, :], scale=1.0 / n).then_inc(ln_done, 1)
                act.wait_ge(ln_done, count)
                if scale_out is None:
                    act.activation(dst, tmp, ACT.Exp, scale=-0.5).then_inc(done, 1)
                else:
                    act.activation(dst, tmp, ACT.Exp, bias=scale_out, scale=-0.5).then_inc(done, 1)

            def x_stats(t, half, par):
                act.wait_ge(x_loaded[par], 32 * (half + 1))
                if not isinstance(t, int) or t >= 2:
                    act.wait_ge(sem["sg_mm"], t - 1)
                    act.wait_ge(sem["xs"], t - 1)
                act.activation(hT[:, par, 0, :, :], x_in[:, par, :].rearrange("p (c k) -> p c k", c=KC), ACT.Square,
                               accum_out=x_ss[:, par:par + 1]).then_inc(sem["x_sq"], 1)
                act.wait_ge(sem["x_sq"], t + 1)
                rsqrt_of(x_r[:, par:par + 1], x_ln[:, :], x_ss[:, par:par + 1], D, sem["x_lnd"], sem["x_rs"], t + 1)

            def split_hi(units):
                for kind, i in units:
                    if (kind, i) == ("in", 0):
                        act.wait_ge(sem["mod_mm"], 5)
                    if (kind, i) == ("out", 0):
                        act.wait_ge(w_split, len(IN_UNITS))
                    n = unit_number(kind, i)
                    slot = UNITS[n][2]
                    col, _, w = IN_UNITS[i] if kind == "in" else (i * UNIT, 0, UNIT)
                    act.wait_ge(staged[slot], 16 * (slot_use(n) + 1))
                    act.activation((w_hi if kind == "in" else wo_hi)[:, :, col:col + w],
                                   slots[slot][:, 0:KC * w].rearrange("p (c n) -> p c n", c=KC),
                                   ACT.Copy, scale=WSCALE).then_inc(w_half, 1)

            act.wait_ge(sem["eps_set"], 2)
            x_stats(0, 0, 0)

            def h_hi(t, par):
                act.wait_ge(sem["h_f32"], t + 1)
                act.activation(hT[:, par, 0, :, :], h_ch, ACT.Copy).then_inc(sem["h_hi"], 1)

            h_hi(0, 0)
            split_hi([("in", i) for i in range(6)])

            def gate_to_stage(count):
                act.wait_ge(sem["gate_bc"], count)
                act.activation(gate_row, pairP[:, :], ACT.Copy).then_inc(sem["gate_row"], 1)

            def program(c):
                t, par = c.t, c.par
                if c.prev:
                    act.wait_ge(sem["o_mm"], t)
                    for hd in range(GH):
                        last = act.activation(junk[:, hd * DV:(hd + 1) * DV], bank7[:, hd * DV:(hd + 1) * DV], ACT.Square,
                                              accum_out=o_ss[:, hd:hd + 1])
                    last.then_inc(sem["o_sq"], 1)
                    act.wait_ge(sem["o_sq"], t)
                    rsqrt_of(o_r[:, :], o_ln[:, :], o_ss[:, :], DV, sem["o_lnd"], sem["o_rs"], t)
                    act.wait_ge(sem["pt_mm"], t)
                    act.activation(probsT, pairP_c, ACT.Copy).then_inc(sem["pt_ev"], 1)
                if c.cur:
                    act.wait_ge(sem["ksg_mm"], t + 1)
                    if c.prev:
                        act.wait_ge(sem["qks_mm"], t)
                    if c.sample:
                        act.wait_ge(sem["out_stored"], 16 * 4)
                    act.activation(ga_tok[:, :], bank5[:, 256:KSG], ACT.Copy, scale=DESCALE)
                    act.activation(qk_tok[:, 4, :], bank5[:, 0:P], ACT.Copy, scale=DESCALE)
                    va = vA_s[0:CHUNK, :] if c.sample else vA[0:CHUNK, par, :]
                    act.activation(va, bank5[0:CHUNK, P:2 * P], ACT.Copy, scale=DESCALE)
                    act.activation(vB[:, par, :], bank5[:, P:2 * P], ACT.Copy, scale=DESCALE).then_inc(sem["ksg_ev"], 1)
                    if c.first:
                        split_hi([("in", 6), ("in", 7)])
                    if c.second:
                        split_hi([("out", 2), ("out", 3)])
                    act.wait_ge(sem["sq_mm"], t + 1)
                    act.activation(qk_tok[:, 0:4, :].rearrange("p b (g k) -> p b g k", g=KVH),
                                   bank7[:, :].rearrange("p (g b k) -> p b g k", g=KVH, b=4),
                                   ACT.Copy, scale=DESCALE).then_inc(sem["sq_ev"], 1)
                    if c.prev:
                        act.wait_ge(sem["pv_mm"], t)
                    act.wait_ge(sem["ksg_ev"], t + 1)
                    act.activation(vA[CHUNK:P, 1 - par, :], vB[CHUNK:P, par, :], ACT.Copy).then_inc(sem["va_prev"], 1)
                    act.wait_ge(sem["gat_mm"], t + 1)
                    if c.first:
                        act.wait_ge(sem["gaT_one"], 1)
                    act.activation(gaT[0:LOWRANK, :], bank5[0:LOWRANK, 0:P], ACT.Copy).then_inc(sem["gat_ev"], 1)
                    if c.first:
                        split_hi([("in", 8), ("in", 9)])
                if c.second:
                    gate_to_stage(1)
                if c.prev:
                    act.wait_ge(sem["mixt_mm"], t)
                    act.activation(mixT[:, 0, :, :], pairP_c, ACT.Copy).then_inc(sem["mixt_hi"], 1)
                if c.cur:
                    act.wait_ge(sem["v_mm"], t + 1)
                    if c.prev:
                        act.wait_ge(sem["u_mm"], t)
                    act.activation(v_tok[:, :], bank6[:, :], ACT.Copy, scale=DESCALE).then_inc(sem["v_ev"], 1)
                    act.wait_ge(sem["z_mm"], t + 1)
                    if c.prev:
                        act.wait_ge(sem["o_mm"], t)
                    act.activation(lsp[:, :, :], z_ch, ACT.Abs).then_inc(sem["z_abs"], 1)
                    act.wait_ge(sem["z_abs"], t + 1)
                    act.activation(lsp[:, :, :], lsp[:, :, :], ACT.Exp, scale=-1.0).then_inc(sem["z_e"], 1)
                    act.wait_ge(sem["z_e"], t + 1)
                    act.activation(lsp[:, :, :], lsp[:, :, :], ACT.Ln, bias=1.0).then_inc(sem["z_l"], 1)
                if c.next:
                    x_stats(t + 1, c.half + par, 1 - par)
                if c.cur:
                    act.wait_ge(sem["bc_d"], t + 1)
                    if c.prev:
                        act.wait_ge(sem["a_mm"], t)
                    act.activation(k_d[:, :, :], q_d[:, :, :], ACT.Exp, scale=-1.0 / TAU).then_inc(sem["e_neg"], 1)
                    act.wait_ge(sem["e_neg"], t + 1)
                    act.activation(q_d[:, :, :], q_d[:, :, :], ACT.Exp, scale=1.0 / TAU).then_inc(sem["e_pos"], 1)
                    act.wait_ge(sem["fac_d"], t + 1)
                    act.activation(fac[:, :, :], fac_in[:, :, :], ACT.Exp, scale=1.0 / TAU).then_inc(sem["fac_e"], 1)
                if c.prev:
                    act.wait_ge(sem["out_mm"], t)
                    if not isinstance(t, int) or t >= 3:
                        act.wait_ge(y_stored[1 - par], 16 * (c.half - (1 - par)))
                    act.activation(y_buf[1 - par], pairP[:, :], ACT.Square, accum_out=y_ss[:, :]).then_inc(sem["y_sq"], 1)
                    act.wait_ge(sem["y_sq"], t)
                    rsqrt_of(y_r[:, :], y_ln[:, :], y_ss[:, :], D * WSCALE * WSCALE, sem["y_lnd"], sem["y_rs"], t, ln_scale[:, :])
                if not c.cur:
                    return
                if c.first:
                    split_hi([("in", 10), ("in", 11)])
                act.wait_ge(sem["m_neg"], t + 1)
                if c.prev:
                    act.wait_ge(sem["pt_mm"], t)
                if c.first:
                    act.wait_ge(sem["zeroed"], 1)
                for g in range(GROUPS):
                    w = CHUNK if c.first and g % 4 < 2 else P
                    act.activation(probs[:, g, 0:w], scores[:, g, 0:w], ACT.Exp, bias=m_neg[:, g:g + 1],
                                   scale=HD ** -0.5, accum_out=row_sum[:, g:g + 1])
                act.wait_ge(sem["sink_d"], t + 1)
                act.activation(sink_e[:, :], sink_d[:, :], ACT.Exp).then_inc(sem["p_exp"], 1)
                act.wait_ge(sem["gg_mm"], t + 1)
                if c.prev:
                    act.wait_ge(sem["sg_g"], t)
                act.activation(etmp[:, :], bank7[:, :], ACT.Exp, scale=-DESCALE).then_inc(sem["gg_e"], 1)
                if c.next:
                    h_hi(t + 1, 1 - par)
                if c.first:
                    split_hi([("out", 0), ("out", 1)])
                if c.sample:
                    gate_to_stage(2)
                act.wait_ge(sem["sg_mm"], t + 1)
                act.wait_ge(sem["gg_x"], t + 1)
                act.activation(etmp[:, :], bank6[:, :], ACT.Exp, scale=-DESCALE).then_inc(sem["sg_e"], 1)

            all_tiles(act, program, 4)

        @block.vector
        def _(dve):
            dve.memset(eps[:, :], EPS).then_inc(sem["eps_set"], 1)
            dve.memset(ln_scale[:, :], -4.1588830833596715).then_inc(sem["eps_set"], 1)
            dve.memset(S_s[:, :, :, :], 0.0).then_inc(sem["ss_zero"], 1)
            dve.memset(vA[CHUNK:P, 0, :], 0.0)
            dve.memset(gaT[:, :], 1.0).then_inc(sem["gaT_one"], 1)
            dve.wait_ge(sem["c_exp"], 1)
            dve.tensor_scalar(c_tmp[:, :, :], c_tmp[:, :, :], 1.0, None, ALU.add).then_inc(sem["c_one"], 1)
            dve.wait_ge(sem["c_one"], 1)
            dve.reciprocal(c_tmp[:, :, :], c_tmp[:, :, :]).then_inc(sem["c_rec"], 1)
            dve.wait_ge(sem["c_rec"], 1)
            dve.tensor_tensor(c_silu[:, :, :].rearrange("p c n -> p n c"), c_tmp[:, :, :], c_ps, ALU.mult)\
               .then_inc(sem["c_silu"], 1)
            dve.wait_ge(sem["bg_t"], 1)
            dve.tensor_copy(bg_col[:, :], bg_ps).then_inc(sem["bg_ev"], 1)

            def rows_to_sbuf(n):
                dve.wait_ge(sem["mod_mm"], 2 * (n + 1))
                dve.tensor_copy(mod_rows[n], rows_ps[n]).then_inc(sem["rows_ev"], 1)

            def split_lo(units):
                for kind, i in units:
                    n = unit_number(kind, i)
                    slot = UNITS[n][2]
                    col, _, w = IN_UNITS[i] if kind == "in" else (i * UNIT, 0, UNIT)
                    hi, lo = (w_hi, w_lo) if kind == "in" else (wo_hi, wo_lo)
                    dve.wait_ge(w_half, split_number(kind, i) + 1)
                    dve.scalar_tensor_tensor(lo[:, :, col:col + w],
                                             slots[slot][:, 0:KC * w].rearrange("p (c n) -> p c n", c=KC), WSCALE,
                                             hi[:, :, col:col + w], ALU.mult, ALU.subtract).then_inc(w_split, 1)

            def h_f32(t, cond):
                dve.wait_ge(sem["xt_mm"], t + 1)
                for cc in range(KC):
                    last = dve.tensor_scalar(h_ch[:, cc, :], pairP_c[:, cc, :], mod[:, KC + cc, cond:cond + 1],
                                             mod[:, cc, cond:cond + 1], ALU.mult, ALU.add)
                last.then_inc(sem["h_f32"], 1)

            def h_lo(t, par):
                dve.wait_ge(sem["h_hi"], t + 1)
                dve.tensor_tensor(hT[:, par, 1, :, :], h_ch, hT[:, par, 0, :, :], ALU.subtract).then_inc(sem["h_lo"], 1)

            def add_bias(first, end):
                dve.tensor_tensor(mod[:, first:end, :], mod_ps[:, first:end, :],
                                  bg_col[:, first:end].unsqueeze(2).to_broadcast([P, end - first, 2]),
                                  ALU.add).then_inc(sem["mod_sum"], 1)

            for n in range(4):
                rows_to_sbuf(n)
            dve.wait_ge(sem["bg_ev"], 1)
            dve.wait_ge(sem["rows_t"], 1)
            add_bias(0, 2 * KC)
            dve.wait_ge(sem["mod_sum"], 1)
            for i in range(2):
                last = dve.scalar_tensor_tensor(mod[:, KC:2 * KC, i], mod[:, KC:2 * KC, i], 1.0,
                                                bg_col[:, 3 * KC:4 * KC], ALU.add, ALU.mult)
            last.then_inc(sem["mod_out"], 1)
            dve.wait_ge(sem["mod_out"], 1)
            h_f32(0, 0)
            rows_to_sbuf(4)
            h_lo(0, 0)
            dve.wait_ge(sem["mod_mm"], 10)
            split_lo([("in", 0)])
            rows_to_sbuf(5)
            dve.wait_ge(sem["causal"], 1)
            dve.wait_ge(sem["kcache_t"], 1)
            dve.tensor_copy(kA_s[:, CHUNK:P], bank4[:, 0:CHUNK]).then_inc(sem["cache_kA"], 1)
            split_lo([("in", 1)])
            dve.wait_ge(sem["rows_t"], 2)
            add_bias(2 * KC, 3 * KC)
            dve.wait_ge(sem["mod_sum"], 2)
            for i in range(2):
                last = dve.tensor_tensor(mod[:, 2 * KC:3 * KC, i], mod[:, 2 * KC:3 * KC, i],
                                         bg_col[:, 4 * KC:5 * KC], ALU.mult)
            last.then_inc(sem["mod_out"], 1)
            split_lo([("in", i) for i in range(2, 6)])

            def gate_diagonal(cond):
                dve.tensor_tensor(gate_diag, ident[:, :].unsqueeze(1).to_broadcast([P, KC, P]),
                                  mod[:, 2 * KC:3 * KC, cond].unsqueeze(2).to_broadcast([P, KC, P]),
                                  ALU.mult).then_inc(sem["gdiag_d"], 1)

            def program(c):
                t, par = c.t, c.par
                if c.prev:
                    dve.wait_ge(sem["o_rs"], t)
                    dve.wait_ge(sem["gg_g"], t)
                    for hd in range(GH):
                        o = slice(hd * DV, (hd + 1) * DV)
                        last = dve.scalar_tensor_tensor(gates[:, o], bank7[:, o], o_r[:, hd:hd + 1], gates[:, o],
                                                        ALU.mult, ALU.mult)
                    last.then_inc(sem["mix_gla"], 1)
                    dve.wait_ge(sem["u_mm"], t)
                    st = S_s if c.after else S
                    for q in range(2):
                        r = slice(DK * q, DK * (q + 1))
                        for b in range(2):
                            last = dve.scalar_tensor_tensor(st[r, b, q, :], st[r, b, q, :], fac[r, b, 5:6],
                                                            u_ps[r, b, :], ALU.mult, ALU.add)
                    last.then_inc(sem["s_upd"], 1)
                if c.second:
                    split_lo([("out", 2), ("out", 3)])
                    dve.wait_ge(sem["mod_out"], 2)
                    dve.wait_ge(w_split, len(IN_UNITS) + OUT_UNITS)
                    gate_diagonal(0)
                if c.first:
                    split_lo([("in", 6), ("in", 7)])
                if c.prev:
                    dve.wait_ge(sem["pv_mm"], t)
                    dve.tensor_tensor(gates[:, 512:1024], bank6[:, :], gates[:, 512:1024], ALU.mult)\
                       .then_inc(sem["mix_swa"], 1)
                if c.first:
                    split_lo([("in", 8), ("in", 9)])
                if c.prev:
                    dve.wait_ge(sem["mixt_hi"], t)
                    dve.tensor_tensor(mixT[:, 1, :, :], pairP_c, mixT[:, 0, :, :], ALU.subtract)\
                       .then_inc(sem["mixt_lo"], 1)
                if c.cur:
                    dve.wait_ge(sem["z_l"], t + 1)
                    if c.prev:
                        dve.wait_ge(sem["a_mm"], t)
                    dve.scalar_tensor_tensor(la[:, :, :], z_ch, 0.0, lsp[:, :, :], ALU.min, ALU.subtract)\
                       .then_inc(sem["la_d"], 1)
                    dve.wait_ge(sem["la_d"], t + 1)
                    dve.tensor_tensor_scan(bsum[:, :, :].rearrange("p b k -> p (b k)"), scan_mask[:, :],
                                           la[:, :, :].rearrange("p b k -> p (b k)"), 0.0, ALU.mult, ALU.add)\
                       .then_inc(sem["scan"], 1)
                    dve.wait_ge(sem["scan"], t + 1)
                    refs = bsum[:, :, :].rearrange("p b (h k) -> p b h k", h=2)[:, :, :, MID0:MID0 + 1]
                    dve.tensor_tensor(q_d[:, :, :].rearrange("p b (h k) -> p b h k", h=2),
                                      bsum[:, :, :].rearrange("p b (h k) -> p b h k", h=2),
                                      refs.to_broadcast([P, 2, 2, CHUNK]), ALU.subtract).then_inc(sem["bc_d"], 1)
                    end = DEC_SEQ - 1 if c.sample else P - 1
                    ref2 = refs.squeeze(3)
                    dve.tensor_copy(fac_in[:, :, 0:2], ref2)
                    dve.tensor_tensor(fac_in[:, :, 2:4], bsum[:, :, end:end + 1].to_broadcast([P, 2, 2]), ref2,
                                      ALU.subtract)
                    dve.tensor_tensor(fac_in[:, :, 4], bsum[:, :, MID1], bsum[:, :, MID0], ALU.subtract)
                    dve.tensor_copy(fac_in[:, :, 5], bsum[:, :, end]).then_inc(sem["fac_d"], 1)
                    dve.wait_ge(sem["qks_mm"], t + 1)
                    dve.tensor_copy(qT[:, :, :, :].rearrange("p c b k -> p b c k"),
                                    pairQ[:, 0:512].rearrange("p (b c k) -> p b c k", b=4, c=2))
                    if c.first:
                        dve.memset(kA[:, 0, CHUNK:P], 0.0)
                    ka = kA_s[:, :] if c.sample else kA[:, par, :]
                    dve.tensor_copy(ka[:, 0:CHUNK], pairQ[:, 512:512 + CHUNK])
                    if c.next:
                        dve.tensor_copy(kA[:, 1 - par, CHUNK:P], pairQ[:, 512 + CHUNK:512 + P])
                    dve.tensor_copy(kB[:, :], pairQ[:, 512:512 + P]).then_inc(sem["qks_ev"], 1)
                    dve.wait_ge(sem["e_pos"], t + 1)
                    dve.scalar_tensor_tensor(q_d[:, :, :], qk_ch[:, 0:2, :], DESCALE * DK ** -0.5, q_d[:, :, :],
                                             ALU.mult, ALU.mult)
                    dve.scalar_tensor_tensor(k_d[:, :, :], qk_ch[:, 2:4, :], DESCALE, k_d[:, :, :],
                                             ALU.mult, ALU.mult).then_inc(sem["qk_d"], 1)
                if c.prev:
                    dve.wait_ge(sem["y_rs"], t)
                    dve.scalar_tensor_tensor(y_buf[1 - par], pairP[:, :], y_r[:, :], gate_row, ALU.mult, ALU.mult)\
                       .then_inc(sem["y_mul"], 1)
                if not c.cur:
                    return
                if c.sample:
                    dve.wait_ge(y_stored[0], 16 * (NT // 2))
                    gate_diagonal(1)
                if c.first:
                    split_lo([("in", 10), ("in", 11)])
                dve.wait_ge(sem["sc_mm"], t + 1)
                if c.first:
                    dve.memset(probs[:, 0:2, CHUNK:P], 0.0)
                    dve.memset(probs[:, 4:6, CHUNK:P], 0.0).then_inc(sem["zeroed"], 1)
                    for g in range(GROUPS):
                        w = CHUNK if g % 4 < 2 else P
                        last = dve.tensor_reduce(smax[:, g:g + 1], scores[:, g, 0:w], AX_X, ALU.max)
                else:
                    dve.tensor_reduce(smax[:, 0:4], scores[:, 0:4, :], AX_X, ALU.max)
                    last = dve.tensor_reduce(smax[:, 4:8], scores[:, 4:8, :], AX_X, ALU.max)
                last.then_inc(sem["smax"], 1)
                dve.wait_ge(sem["smax"], t + 1)
                dve.scalar_tensor_tensor(m_pos[:, :], smax[:, :], HD ** -0.5, sinks[:, :], ALU.mult, ALU.max)\
                   .then_inc(sem["m_pos"], 1)
                dve.wait_ge(sem["m_pos"], t + 1)
                dve.tensor_scalar(m_neg[:, :], m_pos[:, :], -1.0, None, ALU.mult).then_inc(sem["m_neg"], 1)
                dve.tensor_tensor(sink_d[:, :], sinks[:, :], m_pos[:, :], ALU.subtract).then_inc(sem["sink_d"], 1)
                if c.next:
                    h_f32(t + 1, int(c.last))
                dve.wait_ge(sem["a_mm"], t + 1)
                if c.first:
                    dve.memset(aT[64:128, :, :, 0:64], 0.0)
                if c.prev:
                    dve.wait_ge(sem["u_mm"], t)
                for q in range(2):
                    dve.tensor_tensor(aT[0:64, :, q, :], a_ps[q][0:64, :, :],
                                      causal[0:64, :].unsqueeze(1).to_broadcast([64, 2, P]), ALU.mult)
                    dve.tensor_tensor(aT[64:128, :, q, 64:128], a_ps[q][64:128, :, 64:128],
                                      causal[64:128, 64:128].unsqueeze(1).to_broadcast([64, 2, 64]), ALU.mult)
                dve.tensor_copy(k_tok[:, :, :], kt_ps).then_inc(sem["at_d"], 1)
                if c.next:
                    h_lo(t + 1, 1 - par)
                dve.wait_ge(sem["p_exp"], t + 1)
                dve.tensor_tensor(den[:, :], row_sum[:, :], sink_e[:, :], ALU.add).then_inc(sem["den"], 1)
                dve.wait_ge(sem["den"], t + 1)
                dve.reciprocal(rden[:, :], den[:, :]).then_inc(sem["rden"], 1)
                dve.wait_ge(sem["gg_e"], t + 1)
                dve.tensor_scalar(etmp[:, :], etmp[:, :], 1.0, None, ALU.add).then_inc(sem["gg_1"], 1)
                dve.wait_ge(sem["gg_1"], t + 1)
                dve.reciprocal(etmp[:, :], etmp[:, :]).then_inc(sem["gg_r"], 1)
                dve.wait_ge(sem["gg_r"], t + 1)
                dve.scalar_tensor_tensor(gates[:, 0:512], bank7[:, :], DESCALE, etmp[:, :], ALU.mult, ALU.mult)\
                   .then_inc(sem["gg_x"], 1)
                if c.first:
                    split_lo([("out", 0), ("out", 1)])
                dve.wait_ge(sem["sg_e"], t + 1)
                dve.tensor_scalar(etmp[:, :], etmp[:, :], 1.0, None, ALU.add).then_inc(sem["sg_1"], 1)
                dve.wait_ge(sem["sg_1"], t + 1)
                dve.reciprocal(etmp[:, :], etmp[:, :]).then_inc(sem["sg_r"], 1)
                dve.wait_ge(sem["sg_r"], t + 1)
                dve.scalar_tensor_tensor(gates[:, 512:1024], bank6[:, :], DESCALE, etmp[:, :], ALU.mult, ALU.mult)\
                   .then_inc(sem["sg_g"], 1)

            all_tiles(dve, program, 2)

        @block.gpsimd
        def _(pool):
            pool.memset(ident[:, :], 0.0).then_inc(sem["ident_z"], 1)
            pool.memset(causal[:, :], 1.0).then_inc(sem["mask_z"], 1)
            pool.memset(scan_mask[:, :], 1.0).then_inc(sem["scan_z"], 1)
            pool.wait_ge(sem["ident_z"], 1)
            pool.affine_select(out=ident[:, :], in_=ident[:, :], compare_op=ALU.not_equal, fill=1.0, base=0,
                               pattern=[[-1, P]], channel_multiplier=1).then_inc(sem["ident"], 1)
            pool.wait_ge(sem["mask_z"], 1)
            pool.affine_select(out=causal[:, :], in_=causal[:, :], compare_op=ALU.is_ge, fill=0.0, base=0,
                               pattern=[[1, P]], channel_multiplier=-1).then_inc(sem["causal"], 1)
            pool.wait_ge(sem["scan_z"], 1)
            pool.memset(scan_mask[:, 0:2 * P:P], 0.0).then_inc(sem["scan_m"], 1)
            pool.memset(S[:, :, :, :], 0.0).then_inc(sem["scan_m"], 1)

            def norm_x(t, par):
                pool.wait_ge(sem["x_rs"], t + 1)
                if not isinstance(t, int) or t >= 1:
                    pool.wait_ge(sem["h_lo"], t)
                pool.tensor_tensor(xs[:, :], x_in[:, par, :], x_r[:, par:par + 1].to_broadcast([P, D]), ALU.mult)\
                    .then_inc(sem["xs"], 1)

            norm_x(0, 0)

            def program(c):
                t, par = c.t, c.par
                if c.cur:
                    pool.wait_ge(sem["ksg_ev"], t + 1)
                    pool.wait_ge(sem["sq_ev"], t + 1)
                    pool.wait_ge(x_loaded[par], 32 * (c.half + 1))
                    rot = qk_tok[:, :, :].rearrange("p b (g k) -> p (b g) k", g=2)
                    x1, x2 = rot[:, :, 0:ROPE_HALF], rot[:, :, ROPE_HALF:2 * ROPE_HALF]
                    cos = trig_in[:, par, 0:ROPE_HALF].unsqueeze(1).to_broadcast([P, 10, ROPE_HALF])
                    sin = trig_in[:, par, ROPE_HALF:].unsqueeze(1).to_broadcast([P, 10, ROPE_HALF])
                    pool.tensor_tensor(rope_cos[:, :, 0, :], x1, cos, ALU.mult)
                    pool.tensor_tensor(rope_cos[:, :, 1, :], x2, cos, ALU.mult)
                    pool.tensor_tensor(rope_sin[:, :, 0, :], x2, sin, ALU.mult)
                    pool.tensor_tensor(rope_sin[:, :, 1, :], x1, sin, ALU.mult).then_inc(sem["rope_m"], 1)
                    pool.wait_ge(sem["rope_m"], t + 1)
                    pool.tensor_tensor(x1, rope_cos[:, :, 0, :], rope_sin[:, :, 0, :], ALU.subtract)
                    pool.tensor_tensor(x2, rope_cos[:, :, 1, :], rope_sin[:, :, 1, :], ALU.add).then_inc(sem["rope"], 1)
                if c.next:
                    norm_x(t + 1, 1 - par)
                if c.cur:
                    pool.wait_ge(sem["qk_d"], t + 1)
                    pool.wait_ge(sem["fac_e"], t + 1)
                    def halves(a):
                        return a[:, :, :].rearrange("p b (h k) -> p b h k", h=2)
                    pool.tensor_tensor(k_off[:, :, :], k_d[:, :, 0:CHUNK],
                                       fac[:, :, 4:5].to_broadcast([P, 2, CHUNK]), ALU.mult)
                    pool.tensor_tensor(halves(q_int), halves(q_d),
                                       fac[:, :, 0:2].unsqueeze(3).to_broadcast([P, 2, 2, CHUNK]), ALU.mult)
                    pool.tensor_tensor(halves(k_out), halves(k_d),
                                       fac[:, :, 2:4].unsqueeze(3).to_broadcast([P, 2, 2, CHUNK]), ALU.mult)\
                        .then_inc(sem["gla_sc"], 1)
                if c.prev:
                    pool.wait_ge(sem["y_mul"], t)
                    pool.wait_ge(sem["res_copied"], 16 * t)
                    pool.tensor_tensor(y_buf[1 - par], y_buf[1 - par], x_res[:, :], ALU.add).then_inc(sem["y_final"], 1)
                if not c.cur:
                    return
                pool.wait_ge(sem["rden"], t + 1)
                pool.tensor_tensor(probs, probs, rden[:, :].unsqueeze(2).to_broadcast([P, GROUPS, P]), ALU.mult)\
                    .then_inc(sem["probs"], 1)
                pool.wait_ge(sem["gg_x"], t + 1)
                gg = gates[:, 0:512].rearrange("p (h v) -> p h v", h=GH)
                pool.tensor_tensor(gg, gg, gnorm[:, :].unsqueeze(1).to_broadcast([P, GH, DV]), ALU.mult)\
                    .then_inc(sem["gg_g"], 1)

            all_tiles(pool, program, 2)


_INS = ["x_prompt", "x_sample", "c_prompt", "c_sample", "state_gla", "cache_swa_k", "cache_swa_v", "w_ada", "b_ada",
        "g_pre", "g_post", "w_in", "w_alpha", "b_alpha", "gla_norm_g", "swa_sinks", "w_out"]
_OUTS = [(1, SEQ, D), (1, DEC_SEQ, D), (1, 1, GH, DK, DV), (1, 1, P, KVH, HD), (1, 1, P, KVH, HD),
         (1, 1, GH, DK, DV), (1, 1, P, KVH, HD), (1, 1, P, KVH, HD)]


def rotary_table():
    import numpy as np
    inv = np.float32(500000.0) ** (-np.arange(ROPE_HALF, dtype=np.float32) * np.float32(2.0) / np.float32(16.0))
    pos = np.concatenate([np.arange(SEQ), PAST + np.arange(P)]).astype(np.float32)
    ang = (pos[:, None] * inv[None, :]).astype(np.float32)
    return np.concatenate([np.cos(ang), np.sin(ang)], axis=1).astype(np.float32)


def kernel(**inputs):
    import numpy as np
    import concourse.bacc as bacc
    from concourse.bass_utils import run_bass_kernel_spmd as run

    nc = bacc.Bacc("TRN2", target_bir_lowering=False, num_devices=1)
    arrays, args = {}, []
    for name in _INS:
        a = np.ascontiguousarray(inputs[name])
        arrays[f"in_{name}"] = a
        args.append(nc.dram_tensor(f"in_{name}", a.shape, F32, kind="ExternalInput").ap())
    arrays["rotary"] = rotary_table()
    args.append(nc.dram_tensor("rotary", arrays["rotary"].shape, F32, kind="ExternalInput").ap())
    for i, shape in enumerate(_OUTS):
        args.append(nc.dram_tensor(f"out_{i}", shape, F32, kind="ExternalOutput").ap())
    hybrid_layer(nc, *args)
    r = run(nc, [arrays], core_ids=[0])
    return tuple(r.results[0][f"out_{i}"] for i in range(len(_OUTS)))
```

```python
from contextlib import ExitStack

import concourse.bass as bass
from concourse import mybir

F32 = mybir.dt.float32
F16 = mybir.dt.float16
ALU = mybir.AluOpType
ACT = mybir.ActivationFunctionType
AX_X = mybir.AxisListType.X

P = 128
D = 1024
KC = D // P
SEQ, DEC_SEQ, PAST = 4096, 64, 1024
CHUNK = 64
NT = SEQ // P
LOOP_END = NT - 2
EPS = 1e-6
GH, DK, DV = 4, 64, 128
LOWRANK = 16
GA_ROWS = 2 * LOWRANK + 1
TAU = 16.0
HEADS, KVH, HD = 8, 2, 64
ROPE_HALF = HD // 8
GROUPS = 8
WSCALE = 64.0
DESCALE = 1.0 / WSCALE
MID0, MID1 = 32, 96

C_GQ, C_GK, C_GV, C_GG, C_GA, C_SQ, C_SK, C_SV, C_SG, C_END = (
    0, 256, 512, 1024, 1536, 1552, 2064, 2192, 2320, 2832)
W_QK, W_KSG, W_SQ, W_V, W_GG, W_SG = 0, 512, 784, 1296, 1808, 2320
KSG = 272
UNIT = 256
IN_UNITS = [(W_QK, C_GQ, 256), (W_QK + 256, C_GK, 256),
            (W_KSG, C_SK, 256), (W_KSG + 256, C_GA, 16),
            (W_SQ, C_SQ, 256), (W_SQ + 256, C_SQ + 256, 256),
            (W_V, C_GV, 256), (W_V + 256, C_GV + 256, 256),
            (W_GG, C_GG, 256), (W_GG + 256, C_GG + 256, 256),
            (W_SG, C_SG, 256), (W_SG + 256, C_SG + 256, 256)]
ADA_UNITS = 3 * D // UNIT
OUT_UNIT = 128
OUT_UNITS = D // OUT_UNIT
UNITS = [("ada", i, slot) for i, slot in enumerate((7, 8, 9, 10, 11, 12, 13, 14, 15, 16, 0, 1))]
UNITS += [("in", i, slot) for i, slot in enumerate((3, 4, 5, 6, 2, 0, 1, 3, 4, 5, 6, 3))]
UNITS += [("out", i, 17 + i % 3) for i in range(OUT_UNITS)]
SLOTS = 20
SAME_PLACE = {17: (0, 17), 18: (1, 18), 19: (1, 19)}


def slot_use(n):
    return sum(1 for u in UNITS[:n] if u[2] == UNITS[n][2])


def unit_number(kind, i):
    return [u[:2] for u in UNITS].index((kind, i))


def split_number(kind, i):
    return i if kind == "in" else len(IN_UNITS) + i


class Tile:

    def __init__(self, t, half, par):
        peeled = isinstance(t, int)
        self.t, self.half, self.par = t, half, par
        self.prev = not (peeled and t == 0)
        self.cur = not (peeled and t == NT + 1)
        self.next = not (peeled and t >= NT)
        self.first = peeled and t == 0
        self.second = peeled and t == 1
        self.last = peeled and t == NT - 1
        self.sample = peeled and t == NT
        self.after = peeled and t == NT + 1


def hybrid_layer(nc, x_prompt, x_sample, c_prompt, c_sample, state_gla, cache_k, cache_v, w_ada, b_ada, g_pre,
                 g_post, w_in, w_alpha, b_alpha, gla_norm_g, swa_sinks, w_out, trig,
                 y_prompt, y_sample, st_prompt, k_prompt, v_prompt, st_sample, k_sample, v_sample):
    ctx = ExitStack()
    with ctx:
        ctx.enter_context(nc.allow_non_contiguous_dma(reason="small column vectors, once"))

        def sb(name, shape, dt=F32):
            return ctx.enter_context(nc.sbuf_tensor(name, shape, dt))

        def psum(name, shape):
            return ctx.enter_context(nc.psum_tensor(name, shape, F32))

        w_hi = sb("w_hi", [P, KC, C_END], F16)
        w_lo = sb("w_lo", [P, KC, C_END], F16)
        wo_hi = sb("wo_hi", [P, KC, D], F16)
        wo_lo = sb("wo_lo", [P, KC, D], F16)
        stage = sb("stage", [P, 4 * D])
        late = sb("late", [P, 2 * D])
        slots = [stage[:, 0:2 * D], stage[:, 2 * D:4 * D], late[:, :]]
        for home, n in ((wo_lo, 2), (wo_hi, 2), (w_hi, 5), (w_lo, 5)):
            flat = home[:, :, :].rearrange("p c n -> p (c n)").bitcast(F32)
            slots += [flat[:, 2 * D * i:2 * D * (i + 1)] for i in range(n)]
        slots += [stage[:, D * i:D * (i + 1)] for i in (1, 2, 3)]
        gate_row = stage[:, 0:D]
        y_buf = [stage[:, 2 * D:3 * D], stage[:, 3 * D:4 * D]]
        gate_diag = y_buf[0].rearrange("p (c k) -> p c k", c=KC)
        first_diag = late[:, 0:D].rearrange("p (c k) -> p c k", c=KC)
        probs = late[:, 0:D].rearrange("p (g k) -> p g k", g=GROUPS)
        probsT = late[:, D:2 * D].rearrange("p (g k) -> p g k", g=GROUPS)
        mixT = late[:, D:2 * D].bitcast(F16).rearrange("p (s c k) -> p s c k", s=2, c=KC)
        x_in = sb("x_in", [P, 2, D])
        x_res = sb("x_res", [P, D])
        trig_in = sb("trig_in", [P, 2, 2 * ROPE_HALF])
        xs = sb("xs", [P, D])
        h_ch = xs[:, :].rearrange("p (c k) -> p c k", c=KC)
        hT = sb("hT", [P, 2, 2, KC, P], F16)
        v_tok = sb("v_tok", [P, GH * DV])
        qk_tok = sb("qk_tok", [P, 5, P])
        ga_pair = sb("ga_pair", [P, 2 * LOWRANK], F16)
        rope_cos = sb("rope_cos", [P, 10, 2, ROPE_HALF])
        rope_sin = sb("rope_sin", [P, 10, 2, ROPE_HALF])
        qT = sb("qT", [P, 2, HEADS, CHUNK], F16)
        kA = sb("kA", [P, KVH, 2, P], F16)
        kB = sb("kB", [P, KVH, 2, P], F16)
        k_cache = sb("k_cache", [P, KVH, 2, CHUNK], F16)
        ident16 = sb("ident16", [P, P], F16)
        vA = sb("vA", [P, 2, P])
        vA_s = sb("vA_s", [P, P])
        vB = sb("vB", [P, 2, P])
        gates = sb("gates", [P, D])
        etmp = sb("etmp", [P, 512])
        q_pair = etmp[:, :].bitcast(F16).rearrange("p (h s k) -> p h s k", h=HEADS, s=2)
        cache_k_tok = x_res[0:CHUNK, 0:P]
        cache_rows = cache_k_tok.rearrange("p (h k) -> p h k", h=KVH).unsqueeze(2).to_broadcast([CHUNK, KVH, 2, HD])
        heads_tok = qk_tok[:, :, :].rearrange("p b (g k) -> p (b g) k", g=2)
        k_twice = heads_tok[:, 8:10, :].unsqueeze(2).to_broadcast([P, KVH, 2, HD])
        lsp = sb("lsp", [P, 2, P])
        la = sb("la", [P, 2, P])
        bsum = sb("bsum", [P, 2, P])
        q_d = sb("q_d", [P, 2, P])
        k_d = sb("k_d", [P, 2, P])
        q_int, k_out = lsp, la
        k_off = sb("k_off", [P, 2, CHUNK])
        k_tok = sb("k_tok", [P, 2, P])
        aT = sb("aT", [P, 2, 2, P])
        S = sb("S", [P, 2, 2, DV])
        S_s = sb("S_s", [P, 2, 2, DV])
        fac_in = sb("fac_in", [P, 2, 6])
        fac = sb("fac", [P, 2, 6])
        ident = sb("ident", [P, P])
        causal = sb("causal", [P, P])
        scan_mask = sb("scan_mask", [P, 2 * P])
        gnorm = sb("gnorm", [P, DV])
        w_al = sb("w_al", [GA_ROWS, 2, GH * DK], F16)
        w_al_in = x_res[0:GA_ROWS, 2 * P:2 * P + GH * DK]
        gaT = sb("gaT", [GA_ROWS, P], F16)
        sinks = sb("sinks", [P, GROUPS])
        c_tmp = sb("c_tmp", [P, 2, KC])
        c_silu = sb("c_silu", [P, KC, 2])
        bg_col = sb("bg_col", [P, 5 * KC])
        mod = sb("mod", [P, 3 * KC, 2])
        x_ss = sb("x_ss", [P, 2])
        x_ln = sb("x_ln", [P, 1])
        x_r = sb("x_r", [P, 2])
        o_ss = sb("o_ss", [P, 4])
        o_ln = sb("o_ln", [P, 4])
        o_r = sb("o_r", [P, 4])
        y_ss = sb("y_ss", [P, 1])
        y_ln = sb("y_ln", [P, 1])
        y_r = sb("y_r", [P, 1])
        smax = sb("smax", [P, GROUPS])
        m_pos = sb("m_pos", [P, GROUPS])
        m_neg = sb("m_neg", [P, GROUPS])
        sink_d = sb("sink_d", [P, GROUPS])
        sink_e = sb("sink_e", [P, GROUPS])
        row_sum = sb("row_sum", [P, GROUPS])
        den = sb("den", [P, GROUPS])
        rden = sb("rden", [P, GROUPS])
        junk = sb("junk", [P, GH * DV], F16)
        k_pair = junk[:, :].rearrange("p (h s d k) -> p h s d k", h=KVH, s=2, d=2)
        eps = sb("eps", [P, 1])
        ln_scale = sb("ln_scale", [P, 1])

        pairP = psum("pairP", [P, 2 * 512])
        pairQ = psum("pairQ", [P, 2 * 512])
        bank4 = psum("bank4", [P, 512])
        bank5 = psum("bank5", [P, 512])
        bank6 = psum("bank6", [P, 512])
        bank7 = psum("bank7", [P, 512])
        pairP_c = pairP[:, :].rearrange("p (c k) -> p c k", c=KC)
        scores = pairQ[:, :].rearrange("p (g k) -> p g k", g=GROUPS)
        qk_ch = bank4[:, :].rearrange("p (b k) -> p b k", b=4)
        z_ch = bank5[:, 0:256].rearrange("p (b k) -> p b k", b=2)
        a_ps = [bank5[:, 0:256].rearrange("p (b k) -> p b k", b=2), bank4[:, 0:256].rearrange("p (b k) -> p b k", b=2)]
        kt_ps = bank4[:, 256:512].rearrange("p (b k) -> p b k", b=2)
        gaT_ps = bank5[:, :].bitcast(F16)[0:2 * LOWRANK, 0:P]
        pair16 = pairQ[:, :].bitcast(F16)
        q_pair_ps = pair16[:, 0:HEADS * P].rearrange("p (h k) -> p h k", h=HEADS)
        k_pair_ps = pair16[:, HEADS * P:(HEADS + 4) * P].rearrange("p (h s k) -> p h s k", h=KVH, s=2)
        cache_ps = bank4[:, :].bitcast(F16)[:, 0:4 * CHUNK].rearrange("p (h s k) -> p h s k", h=KVH, s=2)
        u_ps = pairQ[:, 640:896].rearrange("p (b k) -> p b k", b=2)
        c_rows, bg_rows = etmp[0:2 * KC, 0:P], etmp[0:5 * KC, P:2 * P]
        c_ps = bank5[:, 64:64 + 2 * KC].rearrange("p (n c) -> p n c", n=2)
        bg_ps = bank5[:, 128:128 + 5 * KC]
        mod_ps = bank5[:, 0:4 * KC].rearrange("p (b c) -> p b c", c=2)
        gate_ps = bank6[:, 0:2 * KC].rearrange("p (b c) -> p b c", c=2)
        rows_ps = [pairQ[0:2, 0:512], pairQ[0:2, 512:1024], bank6[0:2, :], bank7[0:2, :], bank4[0:2, :],
                   pairQ[0:2, 0:512]]
        mod_rows = [gates[0:2, 0:512], gates[0:2, 512:1024], v_tok[0:2, :],
                    qk_tok[0:2, 0:4, :].rearrange("p b k -> p (b k)"),
                    aT[0:2, :, :, :].rearrange("p b q k -> p (b q k)"), etmp[0:2, :]]

        sem = {}
        for name in ("c_load bg_load const_load c_t bg_t bg_ev rows_ev rows_t c_exp c_one c_rec c_silu eps_set "
                     "ident_z ident mask_z causal scan_z scan_m ss_zero gaT_one ga_lo w_al_hi w_al_lo mod_mm "
                     "mod_sum mod_out zeroed kcache_t cache_kA gdiag_d gate_bc gate_row x_sq x_lnd x_rs xs h_f32 "
                     "h_hi h_lo res_copied y_final out_stored qk_mm qk_ev qkt_mm ksg_mm pv_mm sq_mm gat_mm "
                     "mixt_mm v_mm z_mm qks_mm out_mm sc_mm gg_mm xt_mm a_mm sg_mm o_mm u_mm pt_mm ksg_ev sq_ev "
                     "gat_ev pt_ev mixt_hi mixt_lo v_ev pair_hi pair_lo ka_prev k_ev qks_ev cache_hi cache_lo "
                     "ident16 rope_m rope va_prev z_abs z_e z_l la_d scan bc_d fac_d fac_e e_pos e_neg qk_d "
                     "gla_sc at_d s_upd o_sq o_lnd o_rs mix_gla mix_swa smax m_pos m_neg sink_d p_exp den rden "
                     "probs gg_e gg_1 gg_r gg_x gg_g sg_e sg_1 sg_r sg_g y_sq y_lnd y_rs y_mul").split():
            sem[name] = ctx.enter_context(nc.semaphore(name))
        staged = [ctx.enter_context(nc.semaphore(f"staged{i}")) for i in range(SLOTS)]
        x_loaded = [ctx.enter_context(nc.semaphore(f"x_loaded{i}")) for i in range(2)]
        y_stored = [ctx.enter_context(nc.semaphore(f"y_stored{i}")) for i in range(2)]
        w_split = ctx.enter_context(nc.semaphore("w_split"))
        w_half = ctx.enter_context(nc.semaphore("w_half"))

        def all_tiles(eng, program, peel):
            for t in range(peel):
                program(Tile(t, t // 2, t % 2))
            with eng.Fori(peel // 2, LOOP_END // 2) as k:
                program(Tile(k * 2, k, 0))
                program(Tile(k * 2 + 1, k, 1))
            for t in range(LOOP_END, NT + 2):
                program(Tile(t, t // 2, t % 2))

        in_units_before = {W_QK: 2, W_KSG: 4, W_SQ: 6, W_V: 8, W_GG: 10, W_SG: 12}
        block = ctx.enter_context(nc.Block())

        @block.sync
        def _(sp):
            def load_x(t, par):
                if isinstance(t, int) and t == NT:
                    sp.dma_start(x_in[0:DEC_SEQ, par, :], x_sample[0]).then_inc(x_loaded[par], 16)
                else:
                    sp.dma_start(x_in[:, par, :], x_prompt[0, bass.ds(t * P, P), :]).then_inc(x_loaded[par], 16)
                sp.dma_start(trig_in[:, par, :], trig[bass.ds(t * P, P), :]).then_inc(x_loaded[par], 16)

            def load_const(dst, src, loaded):
                sp.dma_start(dst, src).then_inc(sem[loaded], 16)

            def load_constants():
                load_const(gnorm[:, :], gla_norm_g[0].partition_broadcast(P), "const_load")
                for i in range(2):
                    load_const(w_al_in[LOWRANK * i:LOWRANK * (i + 1), :], w_alpha[0], "const_load")
                load_const(w_al_in[2 * LOWRANK:GA_ROWS, :], b_alpha, "const_load")
                load_const(cache_k_tok[:, :], cache_k[0, 0, CHUNK:2 * CHUNK].rearrange("t h d -> t (h d)"),
                           "const_load")
                load_const(vA_s[CHUNK:P, :], cache_v[0, 0, CHUNK:2 * CHUNK].rearrange("t h d -> t (h d)"),
                           "const_load")
                sp.wait_ge(sem["ss_zero"], 1)
                for q in range(2):
                    load_const(S_s[DK * q:DK * q + DK, :, q, :],
                               state_gla[0, 0].rearrange("(b q) k v -> q k b v", q=2)[q], "const_load")
                sink_v = swa_sinks[0].rearrange("(g pp e) -> e g pp", g=KVH, pp=2)
                sink_d4 = sinks[:, :].rearrange("p (g c pp) -> p g c pp", g=KVH, c=2)
                for e in range(2):
                    for g in range(KVH):
                        for ch in range(2):
                            load_const(sink_d4[CHUNK * e:CHUNK * (e + 1), g, ch, :],
                                       sink_v[e, g].partition_broadcast(CHUNK), "const_load")

            for i, cvec in enumerate((c_prompt, c_sample)):
                load_const(c_rows[KC * i:KC * (i + 1), :], cvec.rearrange("o (c p) -> (o c) p", p=P), "c_load")
            for n, (kind, i, slot) in enumerate(UNITS):
                before = [u for u in UNITS[:n] if u[2] in SAME_PLACE.get(slot, (slot,))]
                if before and before[-1][0] == "ada":
                    sp.wait_ge(sem["mod_mm"], before[-1][1] + 1)
                elif before:
                    sp.wait_ge(w_split, split_number(*before[-1][:2]) + 1)
                if kind == "ada":
                    src, w = w_ada[0, :, i * UNIT:(i + 1) * UNIT], UNIT
                elif kind == "in":
                    src, w = w_in[0, :, IN_UNITS[i][1]:IN_UNITS[i][1] + IN_UNITS[i][2]], IN_UNITS[i][2]
                else:
                    src, w = w_out[0, :, i * OUT_UNIT:(i + 1) * OUT_UNIT], OUT_UNIT
                dst = slots[slot][:, 0:KC * w].rearrange("p (c n) -> p c n", c=KC)
                sp.dma_start(dst, src.rearrange("(c p) n -> p c n", p=P)).then_inc(staged[slot], 16)
                if (kind, i) == ("ada", 0):
                    load_x(0, 0)
                    load_const(bg_rows[0:3 * KC, :], b_ada.rearrange("o (c p) -> (o c) p", p=P), "bg_load")
                    for j, g in enumerate((g_pre, g_post)):
                        load_const(bg_rows[(3 + j) * KC:(4 + j) * KC, :], g.rearrange("o (c p) -> (o c) p", p=P),
                                   "bg_load")
                if (kind, i) == ("ada", 9):
                    load_constants()
                if (kind, i) == ("in", 7):
                    load_x(1, 1)
            sp.dma_start(k_sample[0, 0, 0:CHUNK], cache_k[0, 0, CHUNK:2 * CHUNK]).then_inc(sem["out_stored"], 16)
            sp.dma_start(v_sample[0, 0, 0:CHUNK], cache_v[0, 0, CHUNK:2 * CHUNK]).then_inc(sem["out_stored"], 16)

            def program(c):
                if c.prev:
                    sp.wait_ge(sem["y_final"], c.t)
                    src = y_buf[1 - c.par]
                    if c.after:
                        sp.dma_start(y_sample[0], src[0:DEC_SEQ, :]).then_inc(y_stored[1 - c.par], 16)
                    else:
                        sp.dma_start(y_prompt[0, bass.ds((c.t - 1) * P, P), :], src).then_inc(y_stored[1 - c.par], 16)
                if c.cur:
                    sp.wait_ge(x_loaded[c.par], 32 * (c.half + 1))
                    sp.dma_start(x_res[:, :], x_in[:, c.par, :]).then_inc(sem["res_copied"], 16)
                if not isinstance(c.t, int) or c.t + 2 <= NT:
                    sp.wait_ge(sem["res_copied"], 16 * (c.t + 1))
                    sp.wait_ge(sem["xs"], c.t + 1)
                    sp.wait_ge(sem["rope"], c.t + 1)
                    load_x(c.t + 2, c.par)
                if c.last or c.sample:
                    n = P if c.last else DEC_SEQ
                    ko, vo = (k_prompt[0, 0], v_prompt[0, 0]) if c.last else (
                        k_sample[0, 0, CHUNK:], v_sample[0, 0, CHUNK:])
                    sp.wait_ge(sem["rope"], c.t + 1)
                    sp.wait_ge(sem["ksg_ev"], c.t + 1)
                    sp.dma_start(ko.rearrange("t h d -> t (h d)"), qk_tok[0:n, 4, :]).then_inc(sem["out_stored"], 16)
                    sp.dma_start(vo.rearrange("t h d -> t (h d)"), vB[0:n, c.par, :]).then_inc(sem["out_stored"], 16)
                if c.sample or c.after:
                    st, buf = (st_prompt, S) if c.sample else (st_sample, S_s)
                    sp.wait_ge(sem["s_upd"], c.t)
                    for q in range(2):
                        sp.dma_start(st[0, 0].rearrange("(b q) k v -> q k b v", q=2)[q],
                                     buf[DK * q:DK * q + DK, :, q, :]).then_inc(sem["out_stored"], 16)

            all_tiles(sp, program, 2)
            sp.wait_ge(sem["out_stored"], 16 * 10)
            sp.wait_ge(y_stored[0], 16 * (NT // 2 + 1))
            sp.wait_ge(y_stored[1], 16 * (NT // 2))

        @block.tensor
        def _(pe):
            def split_product(out, a, b):
                for c in range(KC):
                    for n, (i, j) in enumerate(((0, 0), (0, 1), (1, 0))):
                        last = pe.matmul(out, a(c, i), b(c, j), start=(c == 0 and n == 0),
                                         stop=(c == KC - 1 and n == 2))
                return last

            def modulation(units):
                for i in units:
                    n = unit_number("ada", i)
                    slot = UNITS[n][2]
                    pe.wait_ge(staged[slot], 16 * (slot_use(n) + 1))
                    w = slots[slot].rearrange("p (c n) -> p c n", c=KC)
                    for c in range(KC):
                        last = pe.matmul(rows_ps[i // 2][:, (i % 2) * UNIT:(i % 2 + 1) * UNIT], c_silu[:, c, :],
                                         w[:, c, :], start=(c == 0), stop=(c == KC - 1))
                    last.then_inc(sem["mod_mm"], 1)

            def rows_to_channels(banks):
                for n in banks:
                    pe.wait_ge(sem["rows_ev"], n + 1)
                    for k in range(4):
                        dst = mod_ps[:, 4 * n + k, :] if n < 4 else gate_ps[:, 4 * (n - 4) + k, :]
                        last = pe.transpose(dst, mod_rows[n][:, k * P:(k + 1) * P],
                                            ident[0:2, 0:2])
                last.then_inc(sem["rows_t"], 1)

            pe.wait_ge(sem["c_load"], 16 * 2)
            pe.wait_ge(sem["ident"], 1)
            pe.transpose(bank5[:, 64:64 + 2 * KC], c_rows, ident[0:2 * KC, 0:2 * KC]).then_inc(sem["c_t"], 1)
            pe.wait_ge(sem["c_silu"], 1)
            modulation(range(1))
            pe.wait_ge(sem["bg_load"], 16 * 3)
            pe.transpose(bg_ps, bg_rows, ident[0:5 * KC, 0:5 * KC]).then_inc(sem["bg_t"], 1)
            modulation(range(1, 4))
            pe.wait_ge(sem["scan_m"], 2)
            pe.wait_ge(sem["xs"], 1)
            for c in range(KC):
                last = pe.transpose(pairP_c[:, c, :], xs[:, c * P:(c + 1) * P], ident[:, :])
            last.then_inc(sem["xt_mm"], 1)
            modulation(range(4, 9))
            rows_to_channels(range(4))
            modulation(range(9, 10))
            pe.wait_ge(sem["rows_ev"], 1)
            modulation(range(10, ADA_UNITS))
            pe.wait_ge(sem["rows_ev"], 5)
            pe.wait_ge(sem["cache_lo"], 1)
            for g in range(KVH):
                for part in range(2):
                    last = pe.transpose(cache_ps[:, g, part, :], k_pair[0:CHUNK, g, part, :, :],
                                        ident16[0:CHUNK, 0:CHUNK])
            last.then_inc(sem["kcache_t"], 1)

            def gate_to_rows(count):
                pe.wait_ge(sem["gdiag_d"], count)
                diagonal = (first_diag, gate_diag)[count - 1]
                for n in range(2):
                    last = pe.matmul(pairP[:, 512 * n:512 * (n + 1)], scan_mask[:, 1:2].to_broadcast([P, P]),
                                     diagonal[:, 4 * n:4 * n + 4, :], start=True, stop=True)
                last.then_inc(sem["gate_bc"], 1)

            def program(c):
                t, par = c.t, c.par

                def h(cc, i):
                    return hT[:, par, i, cc, :]

                def project(bank, width, col, done):
                    if c.first:
                        pe.wait_ge(w_split, in_units_before[col])
                    split_product(bank[:, 0:width], h,
                                  lambda cc, i: (w_hi, w_lo)[i][:, cc, col:col + width]).then_inc(done, 1)

                if c.cur:
                    pe.wait_ge(sem["h_lo"], t + 1)
                    if c.first:
                        pe.wait_ge(sem["cache_kA"], 1)
                    else:
                        pe.wait_ge(sem["at_d"], t)
                    project(bank4, 512, W_QK, sem["qk_mm"])
                    if c.first:
                        rows_to_channels((4, 5))

                def transpose_probs():
                    pe.wait_ge(sem["probs"], t)
                    if c.after:
                        pe.wait_ge(sem["gate_row"], 2)
                    else:
                        pe.wait_ge(sem["h_f32"], t + 1)
                    for g in range(GROUPS):
                        last = pe.transpose(pairP_c[:, g, :], probs[:, g, :], ident[:, :])
                    last.then_inc(sem["pt_mm"], 1)

                if c.after:
                    transpose_probs()
                if c.prev:
                    pe.wait_ge(sem["at_d"], t)
                    pe.wait_ge(sem["gg_x"], t)
                    pe.wait_ge(sem["v_ev"], t)
                    if not c.second:
                        pe.wait_ge(sem["s_upd"], t - 1)
                    st = S_s if c.after else S
                    for b in range(2):
                        pe.matmul(bank7[:, 2 * b * DV:2 * (b + 1) * DV], q_int[:, b, :], st[:, b, :, :],
                                  start=True, stop=False)
                        for q in range(2):
                            o = slice((2 * b + q) * DV, (2 * b + q + 1) * DV)
                            last = pe.matmul(bank7[:, o], aT[:, b, q, :], v_tok[:, o], start=False, stop=(q == 1))
                    last.then_inc(sem["o_mm"], 1)
                    n = DEC_SEQ if c.after else P
                    pe.wait_ge(sem["p_exp"], t)
                    for hd in range(GH):
                        b, q = hd // 2, hd % 2
                        last = pe.matmul(u_ps[DK * q:DK * (q + 1), b, :], k_tok[0:n, b, DK * q:DK * (q + 1)],
                                         v_tok[0:n, hd * DV:(hd + 1) * DV], start=True, stop=True)
                    last.then_inc(sem["u_mm"], 1)
                if c.prev and c.cur:
                    transpose_probs()
                if c.cur:
                    project(bank5, KSG, W_KSG, sem["ksg_mm"])
                if c.prev:
                    pe.wait_ge(sem["pt_ev"], t)
                    pe.wait_ge(sem["sg_g"], t)
                    pe.wait_ge(sem["va_prev"], t)
                    for ch in range(2):
                        vsrc = vB[:, 1 - par, :] if ch else (vA_s[:, :] if c.after else vA[:, 1 - par, :])
                        for head in range(HEADS):
                            g, pp, e = head // 4, head % 4 // 2, head % 2
                            last = pe.matmul(bank6[CHUNK * ch:CHUNK * (ch + 1), head * HD:(head + 1) * HD],
                                             probsT[:, 4 * g + 2 * ch + pp, CHUNK * e:CHUNK * (e + 1)],
                                             vsrc[:, HD * g:HD * (g + 1)], start=True, stop=True)
                    last.then_inc(sem["pv_mm"], 1)
                if c.cur:
                    if c.prev:
                        pe.wait_ge(sem["mix_gla"], t)
                    project(bank7, 512, W_SQ, sem["sq_mm"])
                    pe.wait_ge(sem["qk_ev"], t + 1)
                    for b in range(4):
                        last = pe.transpose(qk_ch[:, b, :], etmp[:, b * P:(b + 1) * P], ident[:, :])
                    last.then_inc(sem["qkt_mm"], 1)
                    pe.wait_ge(sem["ksg_ev"], t + 1)
                    pe.wait_ge(sem["ga_lo"], t + 1)
                    pe.transpose(gaT_ps, ga_pair[:, :], ident16[:, :]).then_inc(sem["gat_mm"], 1)
                if c.prev:
                    pe.wait_ge(sem["mix_gla"], t)
                    for cc in range(KC):
                        if cc == KC // 2:
                            pe.wait_ge(sem["mix_swa"], t)
                        last = pe.transpose(pairP_c[:, cc, :], gates[:, cc * P:(cc + 1) * P], ident[:, :])
                    last.then_inc(sem["mixt_mm"], 1)
                if c.cur:
                    if c.first:
                        pe.wait_ge(sem["mod_sum"], 2)
                    if c.prev:
                        pe.wait_ge(sem["mix_swa"], t)
                    project(bank6, 512, W_V, sem["v_mm"])
                    if c.first:
                        pe.wait_ge(sem["w_al_lo"], 1)
                        pe.wait_ge(sem["gaT_one"], 1)
                    pe.wait_ge(sem["gat_ev"], t + 1)
                    for b in range(2):
                        for part in range(2):
                            last = pe.matmul(z_ch[:, b, :], w_al[:, part, b * P:(b + 1) * P], gaT[:, :],
                                             start=(part == 0), stop=(part == 1))
                    last.then_inc(sem["z_mm"], 1)
                    pe.wait_ge(sem["pair_lo"], t + 1)
                    if c.prev:
                        pe.wait_ge(sem["s_upd"], t)
                    for head in range(HEADS):
                        last = pe.transpose(q_pair_ps[:, head, :], q_pair[:, 2 * (head % 4) + head // 4, :, :],
                                            ident16[:, :])
                    for g in range(KVH):
                        for part in range(2):
                            last = pe.transpose(k_pair_ps[:, g, part, :], k_pair[:, g, part, :, :], ident16[:, :])
                    last.then_inc(sem["qks_mm"], 1)
                if c.prev:
                    pe.wait_ge(sem["mixt_lo"], t)
                    for n in range(2):
                        if c.second:
                            pe.wait_ge(w_split, len(IN_UNITS) + (n + 1) * OUT_UNITS // 2)
                        last = split_product(pairP[:, 512 * n:512 * (n + 1)], lambda cc, i: mixT[:, i, cc, :],
                                             lambda cc, i: (wo_hi, wo_lo)[i][:, cc, 512 * n:512 * (n + 1)])
                    last.then_inc(sem["out_mm"], 1)
                if not c.cur:
                    return
                if c.first:
                    pe.wait_ge(sem["h_f32"], 1)
                    gate_to_rows(1)
                pe.wait_ge(sem["qks_ev"], t + 1)
                pe.wait_ge(sem["k_ev"], t + 1)
                for ch in range(2):
                    for pp in range(2):
                        for g in range(KVH):
                            kk = kB if ch else kA
                            for part in range(2):
                                last = pe.matmul(scores[:, 4 * g + 2 * ch + pp, :],
                                                 qT[:, ch, 4 * g + 2 * pp:4 * g + 2 * pp + 2, :], kk[:, g, part, :],
                                                 start=(part == 0), stop=(part == 1))
                last.then_inc(sem["sc_mm"], 1)
                pe.wait_ge(sem["sq_ev"], t + 1)
                project(bank7, 512, W_GG, sem["gg_mm"])
                if c.sample:
                    pe.wait_ge(sem["y_mul"], t)
                    gate_to_rows(2)
                if c.next:
                    pe.wait_ge(sem["xs"], t + 2)
                    if c.prev:
                        pe.wait_ge(sem["y_mul"], t)
                    else:
                        pe.wait_ge(sem["gate_row"], 1)
                    for cc in range(KC):
                        last = pe.transpose(pairP_c[:, cc, :], xs[:, cc * P:(cc + 1) * P], ident[:, :])
                    last.then_inc(sem["xt_mm"], 1)
                pe.wait_ge(sem["gla_sc"], t + 1)
                for b in range(2):
                    pe.transpose(kt_ps[:, b, :], k_out[:, b, :], ident[:, :])
                for b in range(2):
                    for q in range(2):
                        r = slice(DK * q, DK * (q + 1))
                        pe.matmul(a_ps[q][0:64, b, 0:64], k_d[r, b, 0:64], q_d[r, b, 0:64], start=True, stop=True)
                        pe.matmul(a_ps[q][0:64, b, 64:128], k_off[r, b, :], q_d[r, b, 64:128], start=True, stop=True)
                        last = pe.matmul(a_ps[q][64:128, b, 64:128], k_d[r, b, 64:128], q_d[r, b, 64:128],
                                         start=True, stop=True)
                last.then_inc(sem["a_mm"], 1)
                pe.wait_ge(sem["v_ev"], t + 1)
                project(bank6, 512, W_SG, sem["sg_mm"])

            all_tiles(pe, program, 2)

        @block.scalar
        def _(act):
            act.preload_act_table_set("natural_log_exp_and_others")

            act.wait_ge(sem["c_t"], 1)
            act.activation(c_tmp[:, :, :], c_ps, ACT.Exp, scale=-1.0).then_inc(sem["c_exp"], 1)

            def rsqrt_of(dst, tmp, ssum, n, ln_done, done, count, scale_out=None):
                act.activation(tmp, ssum, ACT.Ln, bias=eps[:, :], scale=1.0 / n).then_inc(ln_done, 1)
                act.wait_ge(ln_done, count)
                if scale_out is None:
                    act.activation(dst, tmp, ACT.Exp, scale=-0.5).then_inc(done, 1)
                else:
                    act.activation(dst, tmp, ACT.Exp, bias=scale_out, scale=-0.5).then_inc(done, 1)

            def x_stats(t, half, par):
                act.wait_ge(x_loaded[par], 32 * (half + 1))
                if not isinstance(t, int) or t >= 2:
                    act.wait_ge(sem["sg_mm"], t - 1)
                    act.wait_ge(sem["xs"], t - 1)
                act.activation(hT[:, par, 0, :, :], x_in[:, par, :].rearrange("p (c k) -> p c k", c=KC), ACT.Square,
                               accum_out=x_ss[:, par:par + 1]).then_inc(sem["x_sq"], 1)
                act.wait_ge(sem["x_sq"], t + 1)
                rsqrt_of(x_r[:, par:par + 1], x_ln[:, :], x_ss[:, par:par + 1], D, sem["x_lnd"], sem["x_rs"], t + 1)

            def split_hi(units):
                for kind, i in units:
                    if (kind, i) == ("in", 0):
                        act.wait_ge(sem["mod_mm"], 5)
                    if (kind, i) == ("out", 0):
                        act.wait_ge(w_split, len(IN_UNITS))
                    n = unit_number(kind, i)
                    slot = UNITS[n][2]
                    col, _, w = IN_UNITS[i] if kind == "in" else (i * OUT_UNIT, 0, OUT_UNIT)
                    act.wait_ge(staged[slot], 16 * (slot_use(n) + 1))
                    act.activation((w_hi if kind == "in" else wo_hi)[:, :, col:col + w],
                                   slots[slot][:, 0:KC * w].rearrange("p (c n) -> p c n", c=KC),
                                   ACT.Copy, scale=WSCALE).then_inc(w_half, 1)

            act.wait_ge(sem["eps_set"], 2)
            x_stats(0, 0, 0)

            def h_hi(t, par):
                act.wait_ge(sem["h_f32"], t + 1)
                act.activation(hT[:, par, 0, :, :], h_ch, ACT.Copy).then_inc(sem["h_hi"], 1)

            act.wait_ge(sem["ident"], 1)
            act.activation(ident16[:, :], ident[:, :], ACT.Copy).then_inc(sem["ident16"], 1)
            act.wait_ge(sem["const_load"], 16 * 16)
            act.activation(k_pair[0:CHUNK, :, 0, :, :], cache_rows, ACT.Copy).then_inc(sem["cache_hi"], 1)
            act.activation(w_al[:, 0, :], w_al_in, ACT.Copy).then_inc(sem["w_al_hi"], 1)
            h_hi(0, 0)
            split_hi([("in", i) for i in range(6)])

            def gate_to_stage(count):
                act.wait_ge(sem["gate_bc"], count)
                if count == 1:
                    act.wait_ge(w_split, split_number("in", 5) + 1)
                act.activation(gate_row, pairP[:, :], ACT.Copy).then_inc(sem["gate_row"], 1)

            def program(c):
                t, par = c.t, c.par
                def copy_probs():
                    act.wait_ge(sem["pt_mm"], t)
                    act.activation(probsT, pairP_c, ACT.Copy).then_inc(sem["pt_ev"], 1)

                if c.after:
                    copy_probs()
                if c.prev:
                    act.wait_ge(sem["o_mm"], t)
                    for hd in range(GH):
                        last = act.activation(junk[:, hd * DV:(hd + 1) * DV], bank7[:, hd * DV:(hd + 1) * DV], ACT.Square,
                                              accum_out=o_ss[:, hd:hd + 1])
                    last.then_inc(sem["o_sq"], 1)
                    act.wait_ge(sem["o_sq"], t)
                    rsqrt_of(o_r[:, :], o_ln[:, :], o_ss[:, :], DV, sem["o_lnd"], sem["o_rs"], t)
                if c.prev and c.cur:
                    copy_probs()
                if c.cur:
                    if c.first:
                        split_hi([("in", 6), ("in", 7)])
                    act.wait_ge(sem["ksg_mm"], t + 1)
                    if c.prev:
                        act.wait_ge(sem["qks_mm"], t)
                    if c.sample:
                        act.wait_ge(sem["out_stored"], 16 * 4)
                    act.activation(ga_pair[:, 0:LOWRANK], bank5[:, 256:KSG], ACT.Copy, scale=DESCALE)
                    act.activation(qk_tok[:, 4, :], bank5[:, 0:P], ACT.Copy, scale=DESCALE)
                    va = vA_s[0:CHUNK, :] if c.sample else vA[0:CHUNK, par, :]
                    act.activation(va, bank5[0:CHUNK, P:2 * P], ACT.Copy, scale=DESCALE)
                    act.activation(vB[:, par, :], bank5[:, P:2 * P], ACT.Copy, scale=DESCALE).then_inc(sem["ksg_ev"], 1)
                    if c.prev:
                        act.wait_ge(sem["sg_g"], t)
                    act.wait_ge(sem["qk_mm"], t + 1)
                    act.activation(etmp[:, :], bank4[:, :], ACT.Copy, scale=DESCALE).then_inc(sem["qk_ev"], 1)
                    act.wait_ge(sem["sq_mm"], t + 1)
                    act.activation(qk_tok[:, 0:4, :].rearrange("p b (g k) -> p b g k", g=KVH),
                                   bank7[:, :].rearrange("p (g b k) -> p b g k", g=KVH, b=4),
                                   ACT.Copy, scale=DESCALE).then_inc(sem["sq_ev"], 1)
                    if c.prev:
                        act.wait_ge(sem["pv_mm"], t)
                    act.wait_ge(sem["ksg_ev"], t + 1)
                    act.activation(vA[CHUNK:P, 1 - par, :], vB[CHUNK:P, par, :], ACT.Copy).then_inc(sem["va_prev"], 1)
                    act.wait_ge(sem["gat_mm"], t + 1)
                    act.activation(gaT[0:2 * LOWRANK, :], gaT_ps, ACT.Copy).then_inc(sem["gat_ev"], 1)
                    if c.second:
                        split_hi([("out", 3), ("out", 4), ("out", 5)])
                    if c.first:
                        split_hi([("in", 8)])
                if c.prev:
                    act.wait_ge(sem["mixt_mm"], t)
                    act.activation(mixT[:, 0, :, :], pairP_c, ACT.Copy).then_inc(sem["mixt_hi"], 1)
                if c.cur:
                    act.wait_ge(sem["rope"], t + 1)
                    act.wait_ge(sem["qkt_mm"], t + 1)
                    act.activation(q_pair[:, :, 0, :], heads_tok[:, 0:8, :], ACT.Copy)
                    act.activation(k_pair[:, :, 0, :, :], k_twice, ACT.Copy).then_inc(sem["pair_hi"], 1)
                    if c.first:
                        split_hi([("in", 9)])
                    if c.second:
                        split_hi([("out", 6), ("out", 7)])
                    act.wait_ge(sem["v_mm"], t + 1)
                    if c.prev:
                        act.wait_ge(sem["u_mm"], t)
                    act.activation(v_tok[:, :], bank6[:, :], ACT.Copy, scale=DESCALE).then_inc(sem["v_ev"], 1)
                    act.wait_ge(sem["z_mm"], t + 1)
                    if c.prev:
                        act.wait_ge(sem["o_mm"], t)
                    act.activation(lsp[:, :, :], z_ch, ACT.Abs).then_inc(sem["z_abs"], 1)
                    act.wait_ge(sem["z_abs"], t + 1)
                    act.activation(lsp[:, :, :], lsp[:, :, :], ACT.Exp, scale=-1.0).then_inc(sem["z_e"], 1)
                    act.wait_ge(sem["z_e"], t + 1)
                    act.activation(lsp[:, :, :], lsp[:, :, :], ACT.Ln, bias=1.0).then_inc(sem["z_l"], 1)
                if c.cur:
                    act.wait_ge(sem["qks_mm"], t + 1)
                    act.activation(qT[:, :, :, :].rearrange("p c h k -> p h c k"),
                                   q_pair_ps.rearrange("p h (c k) -> p h c k", c=2), ACT.Copy)\
                       .then_inc(sem["qks_ev"], 1)
                if c.next:
                    x_stats(t + 1, c.half + par, 1 - par)
                if c.first:
                    split_hi([("in", 10)])
                    gate_to_stage(1)
                if c.cur:
                    act.wait_ge(sem["bc_d"], t + 1)
                    if c.prev:
                        act.wait_ge(sem["a_mm"], t)
                    act.activation(k_d[:, :, :], q_d[:, :, :], ACT.Exp, scale=-1.0 / TAU).then_inc(sem["e_neg"], 1)
                    act.wait_ge(sem["e_neg"], t + 1)
                    act.activation(q_d[:, :, :], q_d[:, :, :], ACT.Exp, scale=1.0 / TAU).then_inc(sem["e_pos"], 1)
                    act.wait_ge(sem["fac_d"], t + 1)
                    act.activation(fac[:, :, :], fac_in[:, :, :], ACT.Exp, scale=1.0 / TAU).then_inc(sem["fac_e"], 1)
                if c.prev:
                    act.wait_ge(sem["out_mm"], t)
                    if not isinstance(t, int) or t >= 3:
                        act.wait_ge(y_stored[1 - par], 16 * (c.half - (1 - par)))
                    act.activation(y_buf[1 - par], pairP[:, :], ACT.Square, accum_out=y_ss[:, :]).then_inc(sem["y_sq"], 1)
                    act.wait_ge(sem["y_sq"], t)
                    rsqrt_of(y_r[:, :], y_ln[:, :], y_ss[:, :], D * WSCALE * WSCALE, sem["y_lnd"], sem["y_rs"], t, ln_scale[:, :])
                if not c.cur:
                    return
                if c.first:
                    split_hi([("in", 11)])
                act.wait_ge(sem["m_neg"], t + 1)
                if c.prev:
                    act.wait_ge(sem["pt_mm"], t)
                if c.first:
                    act.wait_ge(sem["zeroed"], 1)
                for g in range(GROUPS):
                    w = CHUNK if c.first and g % 4 < 2 else P
                    act.activation(probs[:, g, 0:w], scores[:, g, 0:w], ACT.Exp, bias=m_neg[:, g:g + 1],
                                   scale=HD ** -0.5, accum_out=row_sum[:, g:g + 1])
                act.wait_ge(sem["sink_d"], t + 1)
                act.activation(sink_e[:, :], sink_d[:, :], ACT.Exp).then_inc(sem["p_exp"], 1)
                if c.first:
                    h_hi(1, 1)
                act.wait_ge(sem["gg_mm"], t + 1)
                if c.prev:
                    act.wait_ge(sem["sg_g"], t)
                act.activation(etmp[:, :], bank7[:, :], ACT.Exp, scale=-DESCALE).then_inc(sem["gg_e"], 1)
                if c.sample:
                    gate_to_stage(2)
                if c.first:
                    split_hi([("out", 0), ("out", 1), ("out", 2)])
                elif c.next:
                    h_hi(t + 1, 1 - par)
                act.wait_ge(sem["sg_mm"], t + 1)
                act.wait_ge(sem["gg_x"], t + 1)
                act.activation(etmp[:, :], bank6[:, :], ACT.Exp, scale=-DESCALE).then_inc(sem["sg_e"], 1)

            all_tiles(act, program, 4)

        @block.vector
        def _(dve):
            dve.memset(eps[:, :], EPS).then_inc(sem["eps_set"], 1)
            dve.memset(ln_scale[:, :], -4.1588830833596715).then_inc(sem["eps_set"], 1)
            dve.memset(S_s[:, :, :, :], 0.0).then_inc(sem["ss_zero"], 1)
            dve.memset(vA[CHUNK:P, 0, :], 0.0)
            dve.memset(gaT[2 * LOWRANK:GA_ROWS, :], 1.0).then_inc(sem["gaT_one"], 1)
            dve.memset(aT[64:128, :, :, 0:64], 0.0)
            dve.wait_ge(sem["c_exp"], 1)
            dve.tensor_scalar(c_tmp[:, :, :], c_tmp[:, :, :], 1.0, None, ALU.add).then_inc(sem["c_one"], 1)
            dve.wait_ge(sem["c_one"], 1)
            dve.reciprocal(c_tmp[:, :, :], c_tmp[:, :, :]).then_inc(sem["c_rec"], 1)
            dve.wait_ge(sem["c_rec"], 1)
            dve.tensor_tensor(c_silu[:, :, :].rearrange("p c n -> p n c"), c_tmp[:, :, :], c_ps, ALU.mult)\
               .then_inc(sem["c_silu"], 1)
            dve.wait_ge(sem["bg_t"], 1)
            dve.tensor_copy(bg_col[:, :], bg_ps).then_inc(sem["bg_ev"], 1)

            def rows_to_sbuf(n):
                dve.wait_ge(sem["mod_mm"], 2 * (n + 1))
                dve.tensor_copy(mod_rows[n], rows_ps[n]).then_inc(sem["rows_ev"], 1)

            def split_lo(units):
                for kind, i in units:
                    n = unit_number(kind, i)
                    slot = UNITS[n][2]
                    col, _, w = IN_UNITS[i] if kind == "in" else (i * OUT_UNIT, 0, OUT_UNIT)
                    hi, lo = (w_hi, w_lo) if kind == "in" else (wo_hi, wo_lo)
                    dve.wait_ge(w_half, split_number(kind, i) + 1)
                    dve.scalar_tensor_tensor(lo[:, :, col:col + w],
                                             slots[slot][:, 0:KC * w].rearrange("p (c n) -> p c n", c=KC), WSCALE,
                                             hi[:, :, col:col + w], ALU.mult, ALU.subtract).then_inc(w_split, 1)

            def h_f32(t, cond):
                dve.wait_ge(sem["xt_mm"], t + 1)
                for cc in range(KC):
                    last = dve.tensor_scalar(h_ch[:, cc, :], pairP_c[:, cc, :], mod[:, KC + cc, cond:cond + 1],
                                             mod[:, cc, cond:cond + 1], ALU.mult, ALU.add)
                last.then_inc(sem["h_f32"], 1)

            def h_lo(t, par):
                dve.wait_ge(sem["h_hi"], t + 1)
                dve.tensor_tensor(hT[:, par, 1, :, :], h_ch, hT[:, par, 0, :, :], ALU.subtract).then_inc(sem["h_lo"], 1)

            def add_bias(first, end, src):
                dve.tensor_tensor(mod[:, first:end, :], src,
                                  bg_col[:, first:end].unsqueeze(2).to_broadcast([P, end - first, 2]),
                                  ALU.add).then_inc(sem["mod_sum"], 1)

            for n in range(4):
                rows_to_sbuf(n)
            dve.wait_ge(sem["bg_ev"], 1)
            dve.wait_ge(sem["rows_t"], 1)
            add_bias(0, 2 * KC, mod_ps)
            dve.wait_ge(sem["mod_sum"], 1)
            for i in range(2):
                last = dve.scalar_tensor_tensor(mod[:, KC:2 * KC, i], mod[:, KC:2 * KC, i], 1.0,
                                                bg_col[:, 3 * KC:4 * KC], ALU.add, ALU.mult)
            last.then_inc(sem["mod_out"], 1)
            dve.wait_ge(sem["mod_out"], 1)
            h_f32(0, 0)
            rows_to_sbuf(4)
            dve.wait_ge(sem["cache_hi"], 1)
            dve.tensor_tensor(k_pair[0:CHUNK, :, 1, :, :], cache_rows, k_pair[0:CHUNK, :, 0, :, :], ALU.subtract)\
               .then_inc(sem["cache_lo"], 1)
            dve.wait_ge(sem["w_al_hi"], 1)
            dve.tensor_tensor(w_al[:, 1, :], w_al_in, w_al[:, 0, :], ALU.subtract).then_inc(sem["w_al_lo"], 1)
            h_lo(0, 0)
            dve.wait_ge(sem["mod_mm"], 10)
            split_lo([("in", 0), ("in", 1)])
            rows_to_sbuf(5)
            dve.wait_ge(sem["causal"], 1)
            dve.wait_ge(sem["kcache_t"], 1)
            dve.tensor_copy(k_cache[:, :, :, :], cache_ps).then_inc(sem["cache_kA"], 1)
            split_lo([("in", i) for i in range(2, 6)])
            dve.wait_ge(sem["rows_t"], 2)
            add_bias(2 * KC, 3 * KC, gate_ps)
            dve.wait_ge(sem["mod_sum"], 2)
            for i in range(2):
                last = dve.tensor_tensor(mod[:, 2 * KC:3 * KC, i], mod[:, 2 * KC:3 * KC, i],
                                         bg_col[:, 4 * KC:5 * KC], ALU.mult)
            last.then_inc(sem["mod_out"], 1)

            def ga_lo(t):
                dve.wait_ge(sem["ksg_ev"], t + 1)
                dve.scalar_tensor_tensor(ga_pair[:, LOWRANK:2 * LOWRANK], bank5[:, 256:KSG], DESCALE,
                                         ga_pair[:, 0:LOWRANK], ALU.mult, ALU.subtract).then_inc(sem["ga_lo"], 1)

            def gate_diagonal(cond, dst):
                dve.tensor_tensor(dst, ident[:, :].unsqueeze(1).to_broadcast([P, KC, P]),
                                  mod[:, 2 * KC:3 * KC, cond].unsqueeze(2).to_broadcast([P, KC, P]),
                                  ALU.mult).then_inc(sem["gdiag_d"], 1)

            def program(c):
                t, par = c.t, c.par
                if c.prev:
                    dve.wait_ge(sem["o_rs"], t)
                    dve.wait_ge(sem["gg_g"], t)
                    for hd in range(GH):
                        o = slice(hd * DV, (hd + 1) * DV)
                        last = dve.scalar_tensor_tensor(gates[:, o], bank7[:, o], o_r[:, hd:hd + 1], gates[:, o],
                                                        ALU.mult, ALU.mult)
                    last.then_inc(sem["mix_gla"], 1)
                    dve.wait_ge(sem["u_mm"], t)
                    st = S_s if c.after else S
                    for q in range(2):
                        r = slice(DK * q, DK * (q + 1))
                        for b in range(2):
                            last = dve.scalar_tensor_tensor(st[r, b, q, :], st[r, b, q, :], fac[r, b, 5:6],
                                                            u_ps[r, b, :], ALU.mult, ALU.add)
                    last.then_inc(sem["s_upd"], 1)
                if c.prev and c.cur:
                    ga_lo(t)
                if c.second:
                    split_lo([("out", 0), ("out", 1), ("out", 2)])
                if c.first:
                    split_lo([("in", 6), ("in", 7)])
                    ga_lo(t)
                    dve.wait_ge(sem["mod_out"], 2)
                    dve.wait_ge(w_split, split_number("in", 4) + 1)
                    gate_diagonal(0, first_diag)
                if c.prev:
                    dve.wait_ge(sem["pv_mm"], t)
                    dve.tensor_tensor(gates[:, 512:1024], bank6[:, :], gates[:, 512:1024], ALU.mult)\
                       .then_inc(sem["mix_swa"], 1)
                if c.second:
                    split_lo([("out", 3), ("out", 4), ("out", 5)])
                if c.prev:
                    dve.wait_ge(sem["mixt_hi"], t)
                    dve.tensor_tensor(mixT[:, 1, :, :], pairP_c, mixT[:, 0, :, :], ALU.subtract)\
                       .then_inc(sem["mixt_lo"], 1)
                if c.cur:
                    dve.wait_ge(sem["pair_hi"], t + 1)
                    dve.tensor_tensor(q_pair[:, :, 1, :], heads_tok[:, 0:8, :], q_pair[:, :, 0, :], ALU.subtract)
                    dve.tensor_tensor(k_pair[:, :, 1, :, :], k_twice, k_pair[:, :, 0, :, :], ALU.subtract)\
                       .then_inc(sem["pair_lo"], 1)
                    if c.first:
                        split_lo([("in", 8), ("in", 9)])
                    if c.first:
                        dve.memset(kA[:, :, :, CHUNK:P], 0.0).then_inc(sem["ka_prev"], 1)
                    else:
                        dve.wait_ge(sem["sc_mm"], t)
                        dve.wait_ge(sem["k_ev"], t)
                        dve.tensor_copy(kA[:, :, :, CHUNK:P],
                                        k_cache[:, :, :, :] if c.sample else kB[:, :, :, CHUNK:P])\
                           .then_inc(sem["ka_prev"], 1)
                    dve.wait_ge(sem["ka_prev"], t + 1)
                    dve.wait_ge(sem["qks_mm"], t + 1)
                    dve.tensor_copy(kA[:, :, :, 0:CHUNK], k_pair_ps[:, :, :, 0:CHUNK])
                    dve.tensor_copy(kB[:, :, :, :], k_pair_ps).then_inc(sem["k_ev"], 1)
                    if c.second:
                        split_lo([("out", 6), ("out", 7)])
                    dve.wait_ge(sem["z_l"], t + 1)
                    if c.prev:
                        dve.wait_ge(sem["a_mm"], t)
                    dve.scalar_tensor_tensor(la[:, :, :], z_ch, 0.0, lsp[:, :, :], ALU.min, ALU.subtract)\
                       .then_inc(sem["la_d"], 1)
                    dve.wait_ge(sem["la_d"], t + 1)
                    dve.tensor_tensor_scan(bsum[:, :, :].rearrange("p b k -> p (b k)"), scan_mask[:, :],
                                           la[:, :, :].rearrange("p b k -> p (b k)"), 0.0, ALU.mult, ALU.add)\
                       .then_inc(sem["scan"], 1)
                    dve.wait_ge(sem["scan"], t + 1)
                    refs = bsum[:, :, :].rearrange("p b (h k) -> p b h k", h=2)[:, :, :, MID0:MID0 + 1]
                    dve.tensor_tensor(q_d[:, :, :].rearrange("p b (h k) -> p b h k", h=2),
                                      bsum[:, :, :].rearrange("p b (h k) -> p b h k", h=2),
                                      refs.to_broadcast([P, 2, 2, CHUNK]), ALU.subtract).then_inc(sem["bc_d"], 1)
                    end = DEC_SEQ - 1 if c.sample else P - 1
                    ref2 = refs.squeeze(3)
                    dve.tensor_copy(fac_in[:, :, 0:2], ref2)
                    dve.tensor_tensor(fac_in[:, :, 2:4], bsum[:, :, end:end + 1].to_broadcast([P, 2, 2]), ref2,
                                      ALU.subtract)
                    dve.tensor_tensor(fac_in[:, :, 4], bsum[:, :, MID1], bsum[:, :, MID0], ALU.subtract)
                    dve.tensor_copy(fac_in[:, :, 5], bsum[:, :, end]).then_inc(sem["fac_d"], 1)
                    if c.first:
                        split_lo([("in", 10)])
                    dve.wait_ge(sem["qkt_mm"], t + 1)
                    dve.wait_ge(sem["e_pos"], t + 1)
                    dve.scalar_tensor_tensor(q_d[:, :, :], qk_ch[:, 0:2, :], DK ** -0.5, q_d[:, :, :],
                                             ALU.mult, ALU.mult)
                    dve.tensor_tensor(k_d[:, :, :], qk_ch[:, 2:4, :], k_d[:, :, :], ALU.mult).then_inc(sem["qk_d"], 1)
                if c.prev:
                    dve.wait_ge(sem["y_rs"], t)
                    dve.scalar_tensor_tensor(y_buf[1 - par], pairP[:, :], y_r[:, :], gate_row, ALU.mult, ALU.mult)\
                       .then_inc(sem["y_mul"], 1)
                if c.after:
                    dve.wait_ge(sem["y_mul"], t)
                    dve.wait_ge(sem["res_copied"], 16 * t)
                    dve.tensor_tensor(y_buf[1 - par], y_buf[1 - par], x_res[:, :], ALU.add).then_inc(sem["y_final"], 1)
                if not c.cur:
                    return
                if c.sample:
                    dve.wait_ge(y_stored[0], 16 * (NT // 2))
                    gate_diagonal(1, gate_diag)
                if c.first:
                    split_lo([("in", 11)])
                dve.wait_ge(sem["sc_mm"], t + 1)
                if c.first:
                    dve.wait_ge(sem["gate_bc"], 1)
                    dve.memset(probs[:, 0:2, CHUNK:P], 0.0)
                    dve.memset(probs[:, 4:6, CHUNK:P], 0.0).then_inc(sem["zeroed"], 1)
                    for g in range(GROUPS):
                        w = CHUNK if g % 4 < 2 else P
                        last = dve.tensor_reduce(smax[:, g:g + 1], scores[:, g, 0:w], AX_X, ALU.max)
                else:
                    dve.tensor_reduce(smax[:, 0:4], scores[:, 0:4, :], AX_X, ALU.max)
                    last = dve.tensor_reduce(smax[:, 4:8], scores[:, 4:8, :], AX_X, ALU.max)
                last.then_inc(sem["smax"], 1)
                dve.wait_ge(sem["smax"], t + 1)
                dve.scalar_tensor_tensor(m_pos[:, :], smax[:, :], HD ** -0.5, sinks[:, :], ALU.mult, ALU.max)\
                   .then_inc(sem["m_pos"], 1)
                dve.wait_ge(sem["m_pos"], t + 1)
                dve.tensor_scalar(m_neg[:, :], m_pos[:, :], -1.0, None, ALU.mult).then_inc(sem["m_neg"], 1)
                dve.tensor_tensor(sink_d[:, :], sinks[:, :], m_pos[:, :], ALU.subtract).then_inc(sem["sink_d"], 1)
                if c.next:
                    h_f32(t + 1, int(c.last))
                dve.wait_ge(sem["a_mm"], t + 1)
                if c.prev:
                    dve.wait_ge(sem["u_mm"], t)
                for q in range(2):
                    dve.tensor_tensor(aT[0:64, :, q, :], a_ps[q][0:64, :, :],
                                      causal[0:64, :].unsqueeze(1).to_broadcast([64, 2, P]), ALU.mult)
                    dve.tensor_tensor(aT[64:128, :, q, 64:128], a_ps[q][64:128, :, 64:128],
                                      causal[64:128, 64:128].unsqueeze(1).to_broadcast([64, 2, 64]), ALU.mult)
                dve.tensor_copy(k_tok[:, :, :], kt_ps).then_inc(sem["at_d"], 1)
                if c.next:
                    h_lo(t + 1, 1 - par)
                dve.wait_ge(sem["p_exp"], t + 1)
                dve.tensor_tensor(den[:, :], row_sum[:, :], sink_e[:, :], ALU.add).then_inc(sem["den"], 1)
                dve.wait_ge(sem["den"], t + 1)
                dve.reciprocal(rden[:, :], den[:, :]).then_inc(sem["rden"], 1)
                dve.wait_ge(sem["gg_e"], t + 1)
                dve.tensor_scalar(etmp[:, :], etmp[:, :], 1.0, None, ALU.add).then_inc(sem["gg_1"], 1)
                dve.wait_ge(sem["gg_1"], t + 1)
                dve.reciprocal(etmp[:, :], etmp[:, :]).then_inc(sem["gg_r"], 1)
                dve.wait_ge(sem["gg_r"], t + 1)
                dve.scalar_tensor_tensor(gates[:, 0:512], bank7[:, :], DESCALE, etmp[:, :], ALU.mult, ALU.mult)\
                   .then_inc(sem["gg_x"], 1)
                dve.wait_ge(sem["sg_e"], t + 1)
                dve.tensor_scalar(etmp[:, :], etmp[:, :], 1.0, None, ALU.add).then_inc(sem["sg_1"], 1)
                dve.wait_ge(sem["sg_1"], t + 1)
                dve.reciprocal(etmp[:, :], etmp[:, :]).then_inc(sem["sg_r"], 1)
                dve.wait_ge(sem["sg_r"], t + 1)
                dve.scalar_tensor_tensor(gates[:, 512:1024], bank6[:, :], DESCALE, etmp[:, :], ALU.mult, ALU.mult)\
                   .then_inc(sem["sg_g"], 1)

            all_tiles(dve, program, 2)

        @block.gpsimd
        def _(pool):
            pool.memset(ident[:, :], 0.0).then_inc(sem["ident_z"], 1)
            pool.memset(causal[:, :], 1.0).then_inc(sem["mask_z"], 1)
            pool.memset(scan_mask[:, :], 1.0).then_inc(sem["scan_z"], 1)
            pool.wait_ge(sem["ident_z"], 1)
            pool.affine_select(out=ident[:, :], in_=ident[:, :], compare_op=ALU.not_equal, fill=1.0, base=0,
                               pattern=[[-1, P]], channel_multiplier=1).then_inc(sem["ident"], 1)
            pool.wait_ge(sem["mask_z"], 1)
            pool.affine_select(out=causal[:, :], in_=causal[:, :], compare_op=ALU.is_ge, fill=0.0, base=0,
                               pattern=[[1, P]], channel_multiplier=-1).then_inc(sem["causal"], 1)
            pool.wait_ge(sem["scan_z"], 1)
            pool.memset(scan_mask[:, 0:2 * P:P], 0.0).then_inc(sem["scan_m"], 1)
            pool.memset(S[:, :, :, :], 0.0).then_inc(sem["scan_m"], 1)

            def norm_x(t, par):
                pool.wait_ge(sem["x_rs"], t + 1)
                if not isinstance(t, int) or t >= 1:
                    pool.wait_ge(sem["h_lo"], t)
                pool.tensor_tensor(xs[:, :], x_in[:, par, :], x_r[:, par:par + 1].to_broadcast([P, D]), ALU.mult)\
                    .then_inc(sem["xs"], 1)

            norm_x(0, 0)

            def program(c):
                t, par = c.t, c.par
                if c.cur:
                    pool.wait_ge(sem["ksg_ev"], t + 1)
                    pool.wait_ge(sem["sq_ev"], t + 1)
                    pool.wait_ge(x_loaded[par], 32 * (c.half + 1))
                    rot = qk_tok[:, :, :].rearrange("p b (g k) -> p (b g) k", g=2)
                    x1, x2 = rot[:, :, 0:ROPE_HALF], rot[:, :, ROPE_HALF:2 * ROPE_HALF]
                    cos = trig_in[:, par, 0:ROPE_HALF].unsqueeze(1).to_broadcast([P, 10, ROPE_HALF])
                    sin = trig_in[:, par, ROPE_HALF:].unsqueeze(1).to_broadcast([P, 10, ROPE_HALF])
                    pool.tensor_tensor(rope_cos[:, :, 0, :], x1, cos, ALU.mult)
                    pool.tensor_tensor(rope_cos[:, :, 1, :], x2, cos, ALU.mult)
                    pool.tensor_tensor(rope_sin[:, :, 0, :], x2, sin, ALU.mult)
                    pool.tensor_tensor(rope_sin[:, :, 1, :], x1, sin, ALU.mult).then_inc(sem["rope_m"], 1)
                    pool.wait_ge(sem["rope_m"], t + 1)
                    pool.tensor_tensor(x1, rope_cos[:, :, 0, :], rope_sin[:, :, 0, :], ALU.subtract)
                    pool.tensor_tensor(x2, rope_cos[:, :, 1, :], rope_sin[:, :, 1, :], ALU.add).then_inc(sem["rope"], 1)
                if c.next:
                    norm_x(t + 1, 1 - par)
                if c.cur:
                    pool.wait_ge(sem["qk_d"], t + 1)
                    pool.wait_ge(sem["fac_e"], t + 1)
                    def halves(a):
                        return a[:, :, :].rearrange("p b (h k) -> p b h k", h=2)
                    pool.tensor_tensor(k_off[:, :, :], k_d[:, :, 0:CHUNK],
                                       fac[:, :, 4:5].to_broadcast([P, 2, CHUNK]), ALU.mult)
                    pool.tensor_tensor(halves(q_int), halves(q_d),
                                       fac[:, :, 0:2].unsqueeze(3).to_broadcast([P, 2, 2, CHUNK]), ALU.mult)
                    pool.tensor_tensor(halves(k_out), halves(k_d),
                                       fac[:, :, 2:4].unsqueeze(3).to_broadcast([P, 2, 2, CHUNK]), ALU.mult)\
                        .then_inc(sem["gla_sc"], 1)
                if c.prev and c.cur:
                    pool.wait_ge(sem["y_mul"], t)
                    pool.wait_ge(sem["res_copied"], 16 * t)
                    pool.tensor_tensor(y_buf[1 - par], y_buf[1 - par], x_res[:, :], ALU.add).then_inc(sem["y_final"], 1)
                if not c.cur:
                    return
                pool.wait_ge(sem["rden"], t + 1)
                pool.tensor_tensor(probs, probs, rden[:, :].unsqueeze(2).to_broadcast([P, GROUPS, P]), ALU.mult)\
                    .then_inc(sem["probs"], 1)
                pool.wait_ge(sem["gg_x"], t + 1)
                gg = gates[:, 0:512].rearrange("p (h v) -> p h v", h=GH)
                pool.tensor_tensor(gg, gg, gnorm[:, :].unsqueeze(1).to_broadcast([P, GH, DV]), ALU.mult)\
                    .then_inc(sem["gg_g"], 1)

            all_tiles(pool, program, 2)


_INS = ["x_prompt", "x_sample", "c_prompt", "c_sample", "state_gla", "cache_swa_k", "cache_swa_v", "w_ada", "b_ada",
        "g_pre", "g_post", "w_in", "w_alpha", "b_alpha", "gla_norm_g", "swa_sinks", "w_out"]
_OUTS = [(1, SEQ, D), (1, DEC_SEQ, D), (1, 1, GH, DK, DV), (1, 1, P, KVH, HD), (1, 1, P, KVH, HD),
         (1, 1, GH, DK, DV), (1, 1, P, KVH, HD), (1, 1, P, KVH, HD)]


def rotary_table():
    import numpy as np
    inv = np.float32(500000.0) ** (-np.arange(ROPE_HALF, dtype=np.float32) * np.float32(2.0) / np.float32(16.0))
    pos = np.concatenate([np.arange(SEQ), PAST + np.arange(P)]).astype(np.float32)
    ang = (pos[:, None] * inv[None, :]).astype(np.float32)
    return np.concatenate([np.cos(ang), np.sin(ang)], axis=1).astype(np.float32)


def kernel(**inputs):
    import numpy as np
    import concourse.bacc as bacc
    from concourse.bass_utils import run_bass_kernel_spmd as run

    nc = bacc.Bacc("TRN2", target_bir_lowering=False, num_devices=1)
    arrays, args = {}, []
    for name in _INS:
        a = np.ascontiguousarray(inputs[name])
        arrays[f"in_{name}"] = a
        args.append(nc.dram_tensor(f"in_{name}", a.shape, F32, kind="ExternalInput").ap())
    arrays["rotary"] = rotary_table()
    args.append(nc.dram_tensor("rotary", arrays["rotary"].shape, F32, kind="ExternalInput").ap())
    for i, shape in enumerate(_OUTS):
        args.append(nc.dram_tensor(f"out_{i}", shape, F32, kind="ExternalOutput").ap())
    hybrid_layer(nc, *args)
    r = run(nc, [arrays], core_ids=[0])
    return tuple(r.results[0][f"out_{i}"] for i in range(len(_OUTS)))
```
